# Optimizing a Trainium2 kernel written in Bass

```python
import jax, jax.numpy as jnp
from jax import lax
import numpy as np

D_MODEL = 1024
BATCH = 1
SEQ = 512
DEPTH = 1

NSA_HEADS = 8
NSA_KV_HEADS = 2
NSA_HEAD_DIM = 64
NSA_GROUP = NSA_HEADS // NSA_KV_HEADS
NSA_WIDTH = NSA_HEADS * NSA_HEAD_DIM
CMP_BLOCK = 32
CMP_STRIDE = 16
SLC_BLOCK = 64
SLC_TOPK = 16
WINDOW = 512
Q_BLOCK = 128
FORCE_SCORE = 1e4
NEG_INF = -1e30
RWKV_HEADS = 8
RWKV_HEAD_DIM = 64
RWKV_WIDTH = RWKV_HEADS * RWKV_HEAD_DIM
DECAY_RANK = 64
ICLR_RANK = 64
VRES_RANK = 32
GATE_RANK = 128
LNX_EPS = 1e-5 * RWKV_HEAD_DIM
D_FF = 2816
CONV_WIDTH = 3
EPS = 1e-6
NSA_Q_COLS = NSA_WIDTH
NSA_KV_COLS = NSA_KV_HEADS * NSA_HEAD_DIM
NSA_GATE_COLS = NSA_HEADS * 3
RWKV_SPLITS = (RWKV_WIDTH, RWKV_WIDTH, RWKV_WIDTH, DECAY_RANK, ICLR_RANK, GATE_RANK)
RWKV_COLS = sum(RWKV_SPLITS)
MERGE_COLS = 2 * D_MODEL
IN_SPLITS = (NSA_Q_COLS, NSA_KV_COLS, NSA_KV_COLS, NSA_KV_COLS, NSA_KV_COLS, NSA_KV_COLS, NSA_KV_COLS, NSA_GATE_COLS, RWKV_COLS, MERGE_COLS)
IN_COLS = sum(IN_SPLITS)


def _split(z, sizes):
    return jnp.split(z, np.cumsum(sizes)[:-1].tolist(), axis=-1)

def _rms_norm(x, g):
    x32 = x.astype(jnp.float32)
    y = x32 * lax.rsqrt(jnp.mean(x32 * x32, axis=-1, keepdims=True) + EPS)
    return (y * g.astype(jnp.float32)).astype(x.dtype)

def _masked_softmax(s, mask):
    p = jax.nn.softmax(jnp.where(mask, s.astype(jnp.float32), NEG_INF), axis=-1) * mask
    return p.astype(s.dtype)

def _nsa(q, kc, vc, ks, vs, kw, vw, gate_logits, qk_gain, cmp_pe, cmp_w1, cmp_w2):
    B, S, _ = q.shape
    dt = q.dtype
    G, HG, Dh = NSA_KV_HEADS, NSA_GROUP, NSA_HEAD_DIM
    scale = Dh ** -0.5
    qh = _rms_norm(q.reshape(B, S, G, HG, Dh), qk_gain[0]).transpose(0, 2, 3, 1, 4)

    nc = (S - CMP_BLOCK) // CMP_STRIDE + 1
    tok = np.arange(nc)[:, None] * CMP_STRIDE + np.arange(CMP_BLOCK)[None, :]

    def compress(z, pe, w1, w2):
        blocks = z.reshape(B, S, G, Dh)[:, tok] + pe[None, None, :, None, :]
        hid = jax.nn.silu(jnp.einsum('bnlgd,lde->bnge', blocks, w1))
        return jnp.einsum('bnge,ef->bgnf', hid, w2)

    k_cmp = _rms_norm(compress(kc, cmp_pe[0], cmp_w1[0], cmp_w2[0]), qk_gain[1])
    v_cmp = compress(vc, cmp_pe[1], cmp_w1[1], cmp_w2[1])
    cmp_end = jnp.arange(nc) * CMP_STRIDE + CMP_BLOCK - 1

    ns = S // SLC_BLOCK
    n_sel = min(SLC_TOPK, ns)
    k_slc = _rms_norm(ks.reshape(B, S, G, Dh), qk_gain[2]).transpose(0, 2, 1, 3).reshape(B, G, ns, SLC_BLOCK, Dh)
    v_slc = vs.reshape(B, S, G, Dh).transpose(0, 2, 1, 3).reshape(B, G, ns, SLC_BLOCK, Dh)
    n_idx = jnp.arange(nc)[:, None]
    s_idx = jnp.arange(ns)
    overlap = ((n_idx * CMP_STRIDE < (s_idx[None, :] + 1) * SLC_BLOCK)
               & (n_idx * CMP_STRIDE + CMP_BLOCK > s_idx[None, :] * SLC_BLOCK)).astype(jnp.float32)

    pad = ((0, 0), (0, 0), (WINDOW, 0), (0, 0))
    k_win = jnp.pad(_rms_norm(kw.reshape(B, S, G, Dh), qk_gain[3]).transpose(0, 2, 1, 3), pad)
    v_win = jnp.pad(vw.reshape(B, S, G, Dh).transpose(0, 2, 1, 3), pad)

    gates = jax.nn.sigmoid(gate_logits.astype(jnp.float32)).astype(dt)
    gates = gates.reshape(B, S, G, HG, 3).transpose(0, 2, 3, 1, 4)
    bi = jnp.arange(B)[:, None, None, None]
    gi = jnp.arange(G)[None, :, None, None]

    def block(c):
        t0 = c * Q_BLOCK
        t = t0 + jnp.arange(Q_BLOCK)
        qb = lax.dynamic_slice_in_dim(qh, t0, Q_BLOCK, axis=3)
        gb = lax.dynamic_slice_in_dim(gates, t0, Q_BLOCK, axis=3)
        s = jnp.einsum('bghtd,bgnd->bghtn', qb, k_cmp) * scale
        p_cmp = _masked_softmax(s, cmp_end[None, :] <= t[:, None])
        o_cmp = jnp.einsum('bghtn,bgnd->bghtd', p_cmp, v_cmp)
        imp = jnp.einsum('bghtn,ns->bgts', p_cmp.astype(jnp.float32), overlap)
        cur = t // SLC_BLOCK
        forced = (s_idx[None, :] == 0) | (s_idx[None, :] == cur[:, None]) | (s_idx[None, :] == cur[:, None] - 1)
        imp = jnp.where(forced, FORCE_SCORE, imp)
        imp = jnp.where(s_idx[None, :] > cur[:, None], -1.0, imp)
        _, sel = lax.top_k(imp, n_sel)
        k_sel = k_slc[bi, gi, sel].reshape(B, G, Q_BLOCK, n_sel * SLC_BLOCK, Dh)
        v_sel = v_slc[bi, gi, sel].reshape(B, G, Q_BLOCK, n_sel * SLC_BLOCK, Dh)
        pos = (sel[..., None] * SLC_BLOCK + jnp.arange(SLC_BLOCK)).reshape(B, G, Q_BLOCK, n_sel * SLC_BLOCK)
        s = jnp.einsum('bghtd,bgtkd->bghtk', qb, k_sel) * scale
        p_slc = _masked_softmax(s, pos[:, :, None] <= t[:, None])
        o_slc = jnp.einsum('bghtk,bgtkd->bghtd', p_slc, v_sel)
        k_w = lax.dynamic_slice_in_dim(k_win, t0, WINDOW + Q_BLOCK, axis=2)
        v_w = lax.dynamic_slice_in_dim(v_win, t0, WINDOW + Q_BLOCK, axis=2)
        kpos = t0 - WINDOW + jnp.arange(WINDOW + Q_BLOCK)
        dist = t[:, None] - kpos[None, :]
        s = jnp.einsum('bghtd,bgkd->bghtk', qb, k_w) * scale
        p_win = _masked_softmax(s, (kpos[None, :] >= 0) & (dist >= 0) & (dist < WINDOW))
        o_win = jnp.einsum('bghtk,bgkd->bghtd', p_win, v_w)
        return gb[..., 0:1] * o_cmp + gb[..., 1:2] * o_slc + gb[..., 2:3] * o_win

    o = lax.map(block, jnp.arange(S // Q_BLOCK))
    return o.transpose(1, 0, 4, 2, 3, 5).reshape(B, S, NSA_WIDTH)

def _wkv7_scan(r, w, k, v, a, b):
    B, S, H, N = r.shape

    def step(state, inp):
        r_t, w_t, k_t, v_t, a_t, b_t = inp
        sa = jnp.einsum('bhvk,bhk->bhv', state, a_t)
        state = state * w_t[:, :, None, :] + sa[..., None] * b_t[:, :, None, :] + v_t[..., None] * k_t[:, :, None, :]
        return state, jnp.einsum('bhvk,bhk->bhv', state, r_t)

    xs = (jnp.swapaxes(r, 0, 1), jnp.swapaxes(w, 0, 1), jnp.swapaxes(k, 0, 1),
          jnp.swapaxes(v, 0, 1), jnp.swapaxes(a, 0, 1), jnp.swapaxes(b, 0, 1))
    _, y = lax.scan(step, jnp.zeros((B, H, N, N), jnp.float32), xs)
    return jnp.swapaxes(y, 0, 1)

def _rwkv7(z, v_first, vres, mu, w0, w_up, a0, a_up, g_up, k_k, k_a, r_k, ln_w, ln_b):
    B, S, _ = z.shape
    dt = z.dtype
    f32 = jnp.float32
    H, N = RWKV_HEADS, RWKV_HEAD_DIM
    z_prev = jnp.pad(z[:, :-1], ((0, 0), (1, 0), (0, 0)))
    z = z + mu * (z_prev - z)
    r, k, v, wd, ad, gd = _split(z, RWKV_SPLITS)
    if vres is None:
        v_first = v
    else:
        v0, v1, v2 = vres
        v = v + (v_first - v) * jax.nn.sigmoid(v0 + (v @ v1) @ v2)
    w = -jax.nn.softplus(-(w0 + jnp.tanh(wd) @ w_up).astype(f32)) - 0.5
    decay = jnp.exp(-jnp.exp(w))
    a = jax.nn.sigmoid((a0 + ad @ a_up).astype(f32))
    g = jax.nn.sigmoid(gd) @ g_up

    def heads(t):
        return t.astype(f32).reshape(B, S, H, N)

    rh, vh, ah, wh = heads(r), heads(v), heads(a), heads(decay)
    kk = heads(k * k_k)
    kk = kk / jnp.maximum(jnp.sqrt(jnp.sum(kk * kk, axis=-1, keepdims=True)), 1e-12)
    kh = heads(k) * (1.0 + (ah - 1.0) * k_a.astype(f32).reshape(H, N))
    y = _wkv7_scan(rh, wh, kh, vh, -kk, kk * ah)
    mean = jnp.mean(y, axis=-1, keepdims=True)
    var = jnp.mean(jnp.square(y - mean), axis=-1, keepdims=True)
    y = (y - mean) * lax.rsqrt(var + LNX_EPS) * ln_w.astype(f32).reshape(H, N) + ln_b.astype(f32).reshape(H, N)
    y = y + jnp.sum(rh * kh * r_k.astype(f32), axis=-1, keepdims=True) * vh
    return y.reshape(B, S, RWKV_WIDTH).astype(dt) * g, v_first

def _conv_ffn(h, w_up, conv_w, w_down):
    u = h @ w_up
    u = lax.conv_general_dilated(u, conv_w[:, None, :], window_strides=(1,),
                                 padding=((CONV_WIDTH - 1, 0),),
                                 dimension_numbers=('NWC', 'WIO', 'NWC'),
                                 feature_group_count=u.shape[-1])
    a, b = jnp.split(u, 2, axis=-1)
    return (jax.nn.silu(a) * b) @ w_down

def first_inputs(seed: int = 0) -> dict:
    key = jax.random.key(seed)
    k = jax.random.split(key, 32)
    L, D, Dh = DEPTH, D_MODEL, NSA_HEAD_DIM
    f32 = jnp.float32

    def nrm(kk, shape, scale):
        return jax.random.normal(kk, shape, f32) * scale

    def gain(kk, shape):
        return 1.0 + 0.1 * jax.random.normal(kk, shape, f32)

    return {
        'x': nrm(k[0], (BATCH, SEQ, D), 1.0),
        'norm_mix': gain(k[1], (L, D)),
        'norm_ffn': gain(k[2], (L, D)),
        'w_in': nrm(k[3], (L, D, IN_COLS), D ** -0.5),
        'qk_gain': gain(k[4], (L, 4, Dh)),
        'cmp_pe': nrm(k[5], (L, 2, CMP_BLOCK, Dh), 0.1),
        'cmp_w1': nrm(k[6], (L, 2, CMP_BLOCK, Dh, Dh), (CMP_BLOCK * Dh) ** -0.5),
        'cmp_w2': nrm(k[7], (L, 2, Dh, Dh), Dh ** -0.5),
        'rwkv_mu': jax.random.uniform(k[8], (L, RWKV_COLS), f32),
        'rwkv_w0': jax.random.uniform(k[9], (L, RWKV_WIDTH), f32, -3.0, 2.0),
        'rwkv_w_up': nrm(k[10], (L, DECAY_RANK, RWKV_WIDTH), 0.1),
        'rwkv_a0': nrm(k[11], (L, RWKV_WIDTH), 0.5),
        'rwkv_a_up': nrm(k[12], (L, ICLR_RANK, RWKV_WIDTH), ICLR_RANK ** -0.5),
        'rwkv_g_up': nrm(k[13], (L, GATE_RANK, RWKV_WIDTH), GATE_RANK ** -0.5),
        'rwkv_k_k': 0.85 + 0.1 * jax.random.normal(k[14], (L, RWKV_WIDTH), f32),
        'rwkv_k_a': gain(k[15], (L, RWKV_WIDTH)),
        'rwkv_r_k': nrm(k[16], (L, RWKV_HEADS, RWKV_HEAD_DIM), 0.1),
        'rwkv_ln_w': gain(k[17], (L, RWKV_WIDTH)),
        'rwkv_ln_b': nrm(k[18], (L, RWKV_WIDTH), 0.02),
        'vres_v0': nrm(k[19], (L - 1, RWKV_WIDTH), 0.5),
        'vres_v1': nrm(k[20], (L - 1, RWKV_WIDTH, VRES_RANK), RWKV_WIDTH ** -0.5),
        'vres_v2': nrm(k[21], (L - 1, VRES_RANK, RWKV_WIDTH), VRES_RANK ** -0.5),
        'proj_nsa': nrm(k[22], (L, NSA_WIDTH, D), NSA_WIDTH ** -0.5),
        'proj_rwkv': nrm(k[23], (L, RWKV_WIDTH, D), RWKV_WIDTH ** -0.5),
        'w_out': nrm(k[24], (L, D, D), D ** -0.5),
        'ffn_up': nrm(k[25], (L, D, 2 * D_FF), D ** -0.5),
        'ffn_conv': nrm(k[26], (L, CONV_WIDTH, 2 * D_FF), CONV_WIDTH ** -0.5),
        'ffn_down': nrm(k[27], (L, D_FF, D), D_FF ** -0.5),
    }

def first_block(x, norm_mix, norm_ffn, w_in, qk_gain, cmp_pe, cmp_w1, cmp_w2, rwkv_mu, rwkv_w0,
              rwkv_w_up, rwkv_a0, rwkv_a_up, rwkv_g_up, rwkv_k_k, rwkv_k_a, rwkv_r_k, rwkv_ln_w,
              rwkv_ln_b, vres_v0, vres_v1, vres_v2, proj_nsa, proj_rwkv, w_out, ffn_up, ffn_conv,
              ffn_down):
    B, S, D = x.shape
    v_first = None
    for l in range(DEPTH):
        h = _rms_norm(x, norm_mix[l])
        u = h @ w_in[l]
        q, kc, vc, ks, vs, kw, vw, nsa_gl, rw, merge = _split(u, IN_SPLITS)
        o_nsa = _nsa(q, kc, vc, ks, vs, kw, vw, nsa_gl, qk_gain[l], cmp_pe[l], cmp_w1[l], cmp_w2[l])
        vres = None if l == 0 else (vres_v0[l - 1], vres_v1[l - 1], vres_v2[l - 1])
        o_rwkv, v_first = _rwkv7(rw, v_first, vres, rwkv_mu[l], rwkv_w0[l], rwkv_w_up[l], rwkv_a0[l],
                                 rwkv_a_up[l], rwkv_g_up[l], rwkv_k_k[l], rwkv_k_a[l], rwkv_r_k[l],
                                 rwkv_ln_w[l], rwkv_ln_b[l])
        gates = jax.nn.sigmoid(merge.astype(jnp.float32)).astype(x.dtype).reshape(B, S, 2, D)
        y = gates[:, :, 0] * (o_nsa @ proj_nsa[l]) + gates[:, :, 1] * (o_rwkv @ proj_rwkv[l])
        x = x + y @ w_out[l]
        x = x + _conv_ffn(_rms_norm(x, norm_ffn[l]), ffn_up[l], ffn_conv[l], ffn_down[l])
    return x


DILATED_GROUPS = ((128, 1), (512, 4), (2048, 16))
N_ATT_GROUPS = 3
ATT_HEADS_PER_GROUP = 4
ATT_HEAD_DIM = 128
ATT_WIDTH = N_ATT_GROUPS * ATT_HEADS_PER_GROUP * ATT_HEAD_DIM
ATT_OUT_WIDTH = ATT_HEADS_PER_GROUP * ATT_HEAD_DIM
ATT_Q_BLOCK = 128
ROPE_THETA = 500000.0
ROPE_DIMS = ATT_HEAD_DIM // 4
MLSTM_HEADS = 4
MLSTM_WIDTH = D_MODEL
MLSTM_HEAD_DIM = MLSTM_WIDTH // MLSTM_HEADS
MLSTM_CHUNK = 64
CONV_WIDTH_2 = 4
D_FF_2 = ((8 * D_MODEL // 3 + 127) // 128) * 128
RMS_EPS = 1e-6
COL_SIZES = (ATT_WIDTH, ATT_WIDTH, ATT_WIDTH, 2 * MLSTM_WIDTH, MLSTM_WIDTH, MLSTM_WIDTH,
             MLSTM_HEADS, MLSTM_HEADS, D_MODEL, D_MODEL)
IN_WIDTH = 3 * ATT_WIDTH + 4 * MLSTM_WIDTH + 2 * MLSTM_HEADS + 2 * D_MODEL


def rmsnorm(x, g):
    xf = x.astype(jnp.float32)
    y = xf * lax.rsqrt(jnp.mean(xf * xf, axis=-1, keepdims=True) + RMS_EPS)
    return (y * g.astype(jnp.float32)).astype(x.dtype)

def swiglu(x, w_gate, w_up, w_down):
    return (jax.nn.silu(x @ w_gate) * (x @ w_up)) @ w_down

def partial_rope(x, positions):
    half = ROPE_DIMS // 2
    inv_freq = jnp.power(ROPE_THETA, -(jnp.arange(half, dtype=jnp.float32) * 2.0 / ROPE_DIMS))
    ang = positions.astype(jnp.float32)[:, None] * inv_freq[None, :]
    cos, sin = jnp.cos(ang)[:, None, :], jnp.sin(ang)[:, None, :]
    xf = x.astype(jnp.float32)
    x1, x2, xp = xf[..., :half], xf[..., half:ROPE_DIMS], xf[..., ROPE_DIMS:]
    out = jnp.concatenate([x1 * cos - x2 * sin, x2 * cos + x1 * sin, xp], axis=-1)
    return out.astype(x.dtype)

def dilated_window_attention(q, k, v, window, dilation):
    B, S, H, dh = q.shape
    L = S // dilation
    span = window // dilation
    bq = ATT_Q_BLOCK
    nblk = -(-L // bq)
    lp = nblk * bq

    def classes(t, front):
        t = t.reshape(B, L, dilation, H, dh)
        return jnp.pad(t, ((0, 0), (front, lp - L), (0, 0), (0, 0), (0, 0)))

    qb = classes(q, 0).reshape(B, nblk, bq, dilation, H, dh)
    idx = np.arange(nblk)[:, None] * bq + np.arange(bq + span)[None, :]
    kw = classes(k, span)[:, idx]
    vw = classes(v, span)[:, idx]
    s = jnp.einsum('bnirhc,bnjrhc->bnrhij', qb, kw).astype(jnp.float32) * (dh ** -0.5)
    qpos = np.arange(nblk)[:, None, None] * bq + np.arange(bq)[None, :, None]
    kpos = np.arange(nblk)[:, None, None] * bq - span + np.arange(bq + span)[None, None, :]
    dist = qpos - kpos
    valid = (dist >= 0) & (dist <= span) & (kpos >= 0)
    s = jnp.where(valid[None, :, None, None], s, -jnp.inf)
    m = jnp.max(s, axis=-1)
    p = jnp.exp(s - m[..., None])
    l = jnp.sum(p, axis=-1)
    o = jnp.einsum('bnrhij,bnjrhc->bnirhc', p, vw.astype(jnp.float32))
    o = o / jnp.moveaxis(l, -1, 2)[..., None]
    lse = jnp.moveaxis(m + jnp.log(l), -1, 2)
    o = o.reshape(B, lp, dilation, H, dh)[:, :L].reshape(B, S, H, dh)
    lse = lse.reshape(B, lp, dilation, H)[:, :L].reshape(B, S, H)
    return o, lse

def causal_depthwise_conv(x, w, b):
    S, K = x.shape[1], w.shape[0]
    xp = jnp.pad(x, ((0, 0), (K - 1, 0), (0, 0)))
    y = b + w[0] * xp[:, 0:S]
    for j in range(1, K):
        y = y + w[j] * xp[:, j:j + S]
    return y

def mlstm_chunkwise(q, k, v, i_pre, log_f):
    B, S, H, dh = q.shape
    lc = MLSTM_CHUNK
    nc = S // lc

    def chunks(t):
        return t.astype(jnp.float32).reshape(B, nc, lc, H, dh).transpose(1, 0, 3, 2, 4)

    def gchunks(t):
        return t.reshape(B, nc, lc, H).transpose(1, 0, 3, 2)

    qc, kc, vc = chunks(q), chunks(k) * (dh ** -0.5), chunks(v)
    ic, fc = gchunks(i_pre), gchunks(log_f)
    causal = np.tril(np.ones((lc, lc), dtype=bool))

    def step(carry, inp):
        C, n, m = carry
        qt, kt, vt, it, ft = inp
        b = jnp.cumsum(ft, axis=-1)
        D = jnp.where(causal, b[..., :, None] - b[..., None, :] + it[..., None, :], -jnp.inf)
        m_inter = b + m[..., None]
        m_t = jnp.maximum(m_inter, jnp.max(D, axis=-1))
        w = jnp.exp(D - m_t[..., None]) * jnp.einsum('bhtk,bhsk->bhts', qt, kt)
        inter = jnp.exp(m_inter - m_t)
        num = jnp.einsum('bhts,bhsv->bhtv', w, vt) + inter[..., None] * jnp.einsum('bhvk,bhtk->bhtv', C, qt)
        den = jnp.sum(w, axis=-1) + inter * jnp.einsum('bhk,bhtk->bht', n, qt)
        h = num / jnp.maximum(jnp.abs(den), jnp.exp(-m_t))[..., None]
        bl = b[..., -1]
        g = bl[..., None] - b + it
        m_new = jnp.maximum(bl + m, jnp.max(g, axis=-1))
        a = jnp.exp(g - m_new[..., None])
        decay = jnp.exp(bl + m - m_new)
        C_new = decay[..., None, None] * C + jnp.einsum('bhsv,bhsk->bhvk', a[..., None] * vt, kt)
        n_new = decay[..., None] * n + jnp.einsum('bhs,bhsk->bhk', a, kt)
        return (C_new, n_new, m_new), h

    init = (jnp.zeros((B, H, dh, dh), jnp.float32), jnp.zeros((B, H, dh), jnp.float32),
            jnp.zeros((B, H), jnp.float32))
    _, hs = lax.scan(step, init, (qc, kc, vc, ic, fc))
    return hs.transpose(1, 0, 3, 2, 4).reshape(B, S, H, dh)

def hybrid_mixer(h, positions, w_in, conv_w, conv_b, i_bias, f_bias, head_g,
                 w_att_branch, w_mlstm_branch, w_out):
    B, S, _ = h.shape
    proj = h @ w_in
    points = np.cumsum(np.array(COL_SIZES))[:-1].tolist()
    q_a, k_a, v_a, qk_m, v_m, o_m, i_pre, f_pre, g_a, g_m = jnp.split(proj, points, axis=-1)

    nh = N_ATT_GROUPS * ATT_HEADS_PER_GROUP
    q_a = partial_rope(q_a.reshape(B, S, nh, ATT_HEAD_DIM), positions)
    k_a = partial_rope(k_a.reshape(B, S, nh, ATT_HEAD_DIM), positions)
    q_a = q_a.reshape(B, S, N_ATT_GROUPS, ATT_HEADS_PER_GROUP, ATT_HEAD_DIM)
    k_a = k_a.reshape(B, S, N_ATT_GROUPS, ATT_HEADS_PER_GROUP, ATT_HEAD_DIM)
    v_a = v_a.reshape(B, S, N_ATT_GROUPS, ATT_HEADS_PER_GROUP, ATT_HEAD_DIM)
    outs, lses = [], []
    for g, (window, dilation) in enumerate(DILATED_GROUPS):
        o, lse = dilated_window_attention(q_a[:, :, g], k_a[:, :, g], v_a[:, :, g], window, dilation)
        outs.append(o)
        lses.append(lse)
    alpha = jax.nn.softmax(jnp.stack(lses, axis=0), axis=0)
    att = jnp.sum(alpha[..., None] * jnp.stack(outs, axis=0), axis=0)
    att = att.reshape(B, S, ATT_OUT_WIDTH).astype(h.dtype)

    qk = jax.nn.silu(causal_depthwise_conv(qk_m, conv_w, conv_b))
    q_m, k_m = jnp.split(qk, 2, axis=-1)
    shp = (B, S, MLSTM_HEADS, MLSTM_HEAD_DIM)
    ig = i_pre.astype(jnp.float32) + i_bias.astype(jnp.float32)
    lf = jax.nn.log_sigmoid(f_pre.astype(jnp.float32) + f_bias.astype(jnp.float32))
    hm = mlstm_chunkwise(q_m.reshape(shp), k_m.reshape(shp), v_m.reshape(shp), ig, lf)
    hm = hm * lax.rsqrt(jnp.mean(hm * hm, axis=-1, keepdims=True) + RMS_EPS)
    hm = hm * head_g.astype(jnp.float32).reshape(MLSTM_HEADS, MLSTM_HEAD_DIM)
    ml = (jax.nn.sigmoid(o_m.astype(jnp.float32)) * hm.reshape(B, S, MLSTM_WIDTH)).astype(h.dtype)

    merged = jax.nn.sigmoid(g_a) * (att @ w_att_branch) + jax.nn.sigmoid(g_m) * (ml @ w_mlstm_branch)
    return merged @ w_out

def second_inputs(seed: int = 0) -> dict:
    key = jax.random.key(seed)
    ks = jax.random.split(key, 24)
    f32 = jnp.float32

    def dense(k, fan_in, shape):
        return jax.random.normal(k, (DEPTH,) + shape, f32) * (fan_in ** -0.5)

    def gain(k, n):
        return 1.0 + 0.05 * jax.random.normal(k, (DEPTH, n), f32)

    return {
        'x': jax.random.normal(ks[0], (BATCH, SEQ, D_MODEL), f32),
        'ffn1_pre_g': gain(ks[1], D_MODEL),
        'ffn1_w_gate': dense(ks[2], D_MODEL, (D_MODEL, D_FF_2)),
        'ffn1_w_up': dense(ks[3], D_MODEL, (D_MODEL, D_FF_2)),
        'ffn1_w_down': dense(ks[4], D_FF_2, (D_FF_2, D_MODEL)),
        'ffn1_post_g': gain(ks[5], D_MODEL),
        'mix_pre_g': gain(ks[6], D_MODEL),
        'w_in': dense(ks[7], D_MODEL, (D_MODEL, IN_WIDTH)),
        'conv_w': dense(ks[8], CONV_WIDTH_2, (CONV_WIDTH_2, 2 * MLSTM_WIDTH)),
        'conv_b': 0.01 * jax.random.normal(ks[9], (DEPTH, 2 * MLSTM_WIDTH), f32),
        'mlstm_i_bias': 0.1 * jax.random.normal(ks[10], (DEPTH, MLSTM_HEADS), f32),
        'mlstm_f_bias': jnp.linspace(3.0, 6.0, MLSTM_HEADS, dtype=f32)[None, :]
                        + 0.1 * jax.random.normal(ks[11], (DEPTH, MLSTM_HEADS), f32),
        'mlstm_head_g': gain(ks[12], MLSTM_WIDTH),
        'w_att_branch': dense(ks[13], ATT_OUT_WIDTH, (ATT_OUT_WIDTH, D_MODEL)),
        'w_mlstm_branch': dense(ks[14], MLSTM_WIDTH, (MLSTM_WIDTH, D_MODEL)),
        'w_out': dense(ks[15], D_MODEL, (D_MODEL, D_MODEL)),
        'mix_post_g': gain(ks[16], D_MODEL),
        'ffn2_pre_g': gain(ks[17], D_MODEL),
        'ffn2_w_gate': dense(ks[18], D_MODEL, (D_MODEL, D_FF_2)),
        'ffn2_w_up': dense(ks[19], D_MODEL, (D_MODEL, D_FF_2)),
        'ffn2_w_down': dense(ks[20], D_FF_2, (D_FF_2, D_MODEL)),
        'ffn2_post_g': gain(ks[21], D_MODEL),
    }

def second_block(x, ffn1_pre_g, ffn1_w_gate, ffn1_w_up, ffn1_w_down, ffn1_post_g,
              mix_pre_g, w_in, conv_w, conv_b, mlstm_i_bias, mlstm_f_bias, mlstm_head_g,
              w_att_branch, w_mlstm_branch, w_out, mix_post_g,
              ffn2_pre_g, ffn2_w_gate, ffn2_w_up, ffn2_w_down, ffn2_post_g):
    positions = jnp.arange(x.shape[1], dtype=jnp.int32)
    for l in range(DEPTH):
        f = swiglu(rmsnorm(x, ffn1_pre_g[l]), ffn1_w_gate[l], ffn1_w_up[l], ffn1_w_down[l])
        x = x + 0.5 * rmsnorm(f, ffn1_post_g[l])
        y = hybrid_mixer(rmsnorm(x, mix_pre_g[l]), positions, w_in[l], conv_w[l], conv_b[l],
                         mlstm_i_bias[l], mlstm_f_bias[l], mlstm_head_g[l],
                         w_att_branch[l], w_mlstm_branch[l], w_out[l])
        x = x + rmsnorm(y, mix_post_g[l])
        f = swiglu(rmsnorm(x, ffn2_pre_g[l]), ffn2_w_gate[l], ffn2_w_up[l], ffn2_w_down[l])
        x = x + 0.5 * rmsnorm(f, ffn2_post_g[l])
    return x


def setup_inputs(seed=0):
    out = dict(first_inputs(seed))
    for name, value in second_inputs(seed + 1).items():
        if name != "x":
            out[name + "_2"] = value
    return out


def reference(
    x, norm_mix, norm_ffn, w_in, qk_gain, cmp_pe, cmp_w1, cmp_w2, rwkv_mu, rwkv_w0, rwkv_w_up,
    rwkv_a0, rwkv_a_up, rwkv_g_up, rwkv_k_k, rwkv_k_a, rwkv_r_k, rwkv_ln_w, rwkv_ln_b, vres_v0,
    vres_v1, vres_v2, proj_nsa, proj_rwkv, w_out, ffn_up, ffn_conv, ffn_down, ffn1_pre_g_2,
    ffn1_w_gate_2, ffn1_w_up_2, ffn1_w_down_2, ffn1_post_g_2, mix_pre_g_2, w_in_2, conv_w_2,
    conv_b_2, mlstm_i_bias_2, mlstm_f_bias_2, mlstm_head_g_2, w_att_branch_2, w_mlstm_branch_2,
    w_out_2, mix_post_g_2, ffn2_pre_g_2, ffn2_w_gate_2, ffn2_w_up_2, ffn2_w_down_2,
    ffn2_post_g_2,
):
    x = first_block(
        x, norm_mix, norm_ffn, w_in, qk_gain, cmp_pe, cmp_w1, cmp_w2, rwkv_mu, rwkv_w0,
        rwkv_w_up, rwkv_a0, rwkv_a_up, rwkv_g_up, rwkv_k_k, rwkv_k_a, rwkv_r_k, rwkv_ln_w,
        rwkv_ln_b, vres_v0, vres_v1, vres_v2, proj_nsa, proj_rwkv, w_out, ffn_up, ffn_conv,
        ffn_down,
    )
    return second_block(
        x, ffn1_pre_g_2, ffn1_w_gate_2, ffn1_w_up_2, ffn1_w_down_2, ffn1_post_g_2, mix_pre_g_2,
        w_in_2, conv_w_2, conv_b_2, mlstm_i_bias_2, mlstm_f_bias_2, mlstm_head_g_2,
        w_att_branch_2, w_mlstm_branch_2, w_out_2, mix_post_g_2, ffn2_pre_g_2, ffn2_w_gate_2,
        ffn2_w_up_2, ffn2_w_down_2, ffn2_post_g_2,
    )


_drawn_inputs = setup_inputs


def setup_inputs(seed=0):
    import zlib

    import numpy as np

    out = dict(_drawn_inputs(seed))
    spreads = {}
    factors = {'qk_gain': 3.752,
     'rwkv_k_k': 14.975,
     'rwkv_ln_b': 3.709,
     'conv_b_2': 8.0,
     'mlstm_i_bias_2': 64.0,
     'ffn2_pre_g_2': 2.734,
     'ffn2_post_g_2': 3.935}
    for name, (base, spread) in spreads.items():
        noise = np.random.default_rng([zlib.crc32(name.encode()), seed]).standard_normal(out[name].shape)
        drawn = base * np.exp(spread * noise) if base else spread * noise
        out[name] = __import__('jax').numpy.asarray(drawn.astype(out[name].dtype))
    for name, factor in factors.items():
        out[name] = (out[name] * factor).astype(out[name].dtype)
    return out
```

```python
from contextlib import ExitStack

import numpy as np
import concourse.bass as bass
from concourse import mybir

F32 = mybir.dt.float32
F32R = mybir.dt.float32r
ACT = mybir.ActivationFunctionType
ALU = mybir.AluOpType
AX = mybir.AxisListType

T = 512
D = 1024
KD = D // 128
FF = 2816
KF = FF // 128
TB = T // 128
EPS = 1e-6
NEG = -1e30

NH, NG, DH = 8, 2, 64
NC = 31
A_UNITS = 11
R_TILES = 14
M_TILES = 16
LNX_EPS = 1e-5 * 64
DECAY = float(np.exp(-0.5))

STAGES = [("nsa", A_UNITS), ("rwkv_merge", R_TILES + M_TILES), ("proj", 8), ("out1", 8),
          ("up1", 2 * KF), ("down1", 24), ("up2", 2 * KF), ("down2", 24),
          ("mix", 85), ("branch", 12), ("out2", 8), ("up3", 2 * KF), ("down3", 24)]
FIRST = {}
_n = 0
for _name, _count in STAGES:
    FIRST[_name] = _n
    _n += _count
UNITS = _n

PARAMS = [("norm_mix", 8), ("norm_ffn", 8), ("mu", 14), ("w0", 4), ("a0", 4), ("k_k", 4), ("k_a", 4),
          ("r_k", 4), ("ln_w", 4), ("ln_b", 4), ("qk_gain", 4), ("ffn_conv", 3 * 2 * KF),
          ("ffn1_pre", 8), ("ffn1_post", 8), ("mix_pre", 8), ("conv_w", 64), ("conv_b", 16),
          ("head_g", 8), ("mix_post", 8), ("ffn2_pre", 8), ("ffn2_post", 8)]
COL = {}
_n = 0
for _name, _count in PARAMS:
    COL[_name] = _n
    _n += _count
NPAR = _n


PREP = 12


class Index:

    def __init__(self, at, turn=None, per=0):
        assert per % 2 == 0
        self.at, self.turn, self.per = at, turn, per
        self.slot = at % 2

    def value(self, more=0):
        n = self.at + more
        return n if self.turn is None else self.turn * self.per + n

    def half(self):
        n = self.at // 2
        return n if self.turn is None else self.turn * (self.per // 2) + n

    def __add__(self, n):
        return Index(self.at + n, self.turn, self.per)


def build_program(nc, io):
    ctx = ExitStack()

    def sb(name, shape, dt=F32, scope=ctx):
        return scope.enter_context(nc.sbuf_tensor(name, shape, dt))

    sems = {}

    def sem(name):
        if name not in sems:
            sems[name] = ctx.enter_context(nc.semaphore(name))
        return sems[name]

    with ctx:
        raw = sb("raw", [128, 2, 1024])
        w_hi = sb("w_hi", [128, 2, 1024], F32R)
        w_lo = sb("w_lo", [128, 2, 1024], F32R)
        x = sb("x", [128, KD, T])
        h_hi = sb("h_hi", [128, KD, T], F32R)
        h_lo = sb("h_lo", [128, KD, T], F32R)
        tmp = sb("tmp", [128, 8, T])
        par = sb("par", [128, NPAR])
        ident = sb("ident", [128, 128])
        blk64 = sb("blk64", [128, 128])
        idd = sb("idd", [128, 64])
        sel = sb("sel", [128, 8])
        eps, lnx_eps = sel[:, 3:4], sel[:, 4:5]
        psum = ctx.enter_context(nc.psum_tensor("psum", [128, 8, 512], F32))

        z1 = ExitStack()
        zm = sb("zm", [128, R_TILES + M_TILES, T + 1], scope=z1)
        masks1 = sb("masks1", [128, 512 + 128 + 128 + 512 + 256], scope=z1)
        causal = masks1[:, 0:512]
        cmp_add = masks1[:, 512:640].rearrange("p (b n) -> p b n", b=TB)
        cmp_mul = masks1[:, 640:768].rearrange("p (b n) -> p b n", b=TB)
        pair_mask = masks1[:, 768:1280]
        sub_mask = masks1[:, 1280:1536].rearrange("p (a n) -> p a n", a=2)
        nsa = ExitStack()
        u = sb("u", [128, A_UNITS, T], scope=nsa)
        blocks = sb("blocks", [128, 2, 32, NC + 1], scope=nsa)
        att_s = blocks[:, 0].rearrange("p l n -> p (l n)")
        att_pt = blocks[:, 1].rearrange("p l n -> p (l n)")
        s_slc, s_win = att_s[:, 0:512], att_s[:, 512:1024]
        pt_slc, pt_win = att_pt[:, 0:512], att_pt[:, 512:1024]
        s_cmp = sb("s_cmp", [128, 32], scope=nsa)
        pt_cmp = sb("pt_cmp", [32, 128], scope=nsa)
        q_st = sb("q_st", [128, T], scope=nsa)
        v_slc = sb("v_slc", [128, TB, 128], scope=nsa)
        v_win = sb("v_win", [128, TB, 128], scope=nsa)
        v_cmp = sb("v_cmp", [32, 128], scope=nsa)
        k_cmp = sb("k_cmp", [128, 3, 32], scope=nsa)
        hid_cmp = sb("hid_cmp", [128, 2, 32], scope=nsa)
        gate_tm = sb("gate_tm", [128, TB, 24], scope=nsa)
        gate_st = sb("gate_st", [128, TB, 2, 3], scope=nsa)
        rq = sb("rq", [128, 48], scope=nsa)
        q_scale = sb("q_scale", [128, 8], scope=nsa)
        gain = sb("gain", [128, 4], scope=nsa)
        soft = sb("soft", [128, 16], scope=nsa)
        cmp_w2 = sb("cmp_w2", [128, 2, 64], scope=nsa)
        cmp_pe = sb("cmp_pe", [128, 2, 32], scope=nsa)
        cmp_w1 = tmp[:, :, :].rearrange("p a t -> p (a t)").rearrange("p (c l e) -> p c l e", c=2, l=32)
        o_nsa, o_rwkv = x[:, 0:4], x[:, 4:8]
        nsa.close()
        rw = ExitStack()
        a_t = sb("a_t", [128, 4, T], scope=rw)
        dw = sb("dw", [128, 4, T], scope=rw)
        g_t = sb("g_t", [128, 4, T], scope=rw)
        lora = sb("lora", [128, 2, 512], scope=rw)
        ar = sb("ar", [128, TB, 2, 128], scope=rw)
        tm0 = sb("tm", [128, 4, 128], scope=rw)
        sc0 = sb("sc", [128, 2, 512], scope=rw)
        dd = sb("dd", [128, 2, 2, 128], scope=rw)
        de = sb("de", [128, 2, 2, 128], scope=rw)
        dm0 = sb("dm", [128, 2, 128], scope=rw)
        wm0 = sb("wm", [128, 2, 256], scope=rw)
        tms = (tm0[:], causal.rearrange("p (a n) -> p a n", a=4))
        scs = (sc0[:], lora[:])
        dms = (dm0[:], masks1[:, 512:768].rearrange("p (a n) -> p a n", a=2))
        wms = (wm0[:], dw[:, 0].rearrange("p (a n) -> p a n", a=2))
        gt = sb("gt", [128, 128], scope=rw)
        pt = sb("pt", [128, 2, 64], scope=rw)
        ql = sb("ql", [128, 2, 64], scope=rw)
        st = sb("st", [128, 2, 64], scope=rw)
        omm = sb("omm", [128, 20], scope=rw)
        rs = sb("rs", [128, 16], scope=rw)
        l_t, li, kk, bt, kt, vt, kh, rk = [tmp[:, n] for n in range(8)]
        rw.close()
        ys = ExitStack()
        y_hi = sb("y_hi", [128, KD, T], F32R, scope=ys)
        y_lo = sb("y_lo", [128, KD, T], F32R, scope=ys)
        ys.close()
        z1.close()
        ffn = ExitStack()
        sqz = sb("sqz", [128, KD, T], scope=ffn)
        hid_hi = sb("hid_hi", [128, KF, T], F32R, scope=ffn)
        hid_lo = sb("hid_lo", [128, KF, T], F32R, scope=ffn)
        ffn.close()
        z2 = ExitStack()
        gates = sb("gates", [128, 16, T], scope=z2)
        att_o = sb("att_o", [128, 4, T], scope=z2)
        mo = sb("mo", [128, KD, T], scope=z2)
        mask_t = sb("mask_t", [128, 128], scope=z2)
        ones128 = sb("ones128", [128, 128], scope=z2)
        par_if = sb("par_if", [4, 2], scope=z2)
        att = ExitStack()
        qk_st = sb("qk_st", [128, 6, T], scope=att)
        v_tm = sb("v_tm", [128, 3, TB, 128], scope=att)
        rope = sb("rope", [32, 2, T], scope=att)
        rope_t = sb("rope_t", [32, T], scope=att)
        rmat = sb("rmat", [128, 32], scope=att)
        mask2 = sb("mask2", [128, 4, 768], scope=att)
        att_p = sb("att_p", [128, 768], scope=att)
        att_pT = sb("att_pT", [128, 768], scope=att)
        att_small = sb("att_small", [128, 8], scope=att)
        att.close()
        ml = ExitStack()
        ml_qk = sb("ml_qk", [128, 4, T], scope=ml)
        ml_v = sb("ml_v", [128, TB, 256], scope=ml)
        ml_o = sb("ml_o", [128, 2, T], scope=ml)
        ml_e = sb("ml_e", [128, 1280], scope=ml)
        ml_w = sb("ml_w", [128, 1280], scope=ml)
        ml_hm = sb("ml_hm", [128, 2, T], scope=ml)
        ml_sq = sb("ml_sq", [128, 2, T], scope=ml)
        ml_d = sb("ml_d", [128, T], scope=ml)
        ml_abs = sb("ml_abs", [128, T], scope=ml)
        ml_small = sb("ml_small", [128, 8], scope=ml)
        c_row = sb("c_row", [4, T], scope=ml)
        nmu_row = sb("nmu_row", [4, T], scope=ml)
        em_row = sb("em_row", [4, T], scope=ml)
        sel4 = sb("sel4", [4, 4, T], scope=ml)
        selh = sb("selh", [4, T], scope=ml)
        rows, b_row, zero_row = tmp[0:4, 0:4], tmp[0:4, 6], tmp[0:4, 7]
        ml.close()
        br = ExitStack()
        ah_hi = sb("ah_hi", [128, 4, T], F32R, scope=br)
        ah_lo = sb("ah_lo", [128, 4, T], F32R, scope=br)
        y2_hi = sb("y2_hi", [128, KD, T], F32R, scope=br)
        y2_lo = sb("y2_lo", [128, KD, T], F32R, scope=br)
        br.close()
        z2.close()

        block = ctx.enter_context(nc.Block())
        p2 = psum[:, 2]
        p3 = psum[:, 3]
        p4 = psum[:, 4]
        p5 = psum[:, 5]
        p6 = psum[:, 6]
        p7 = psum[:, 7]
        ML_AT = ((0, 512), (512, 896), (1024, 1280), (896, 1024))
        ml_e_ps = (psum[:, 2], psum[:, 3, 0:384], psum[:, 4, 0:256], psum[:, 3, 384:512])
        ml_s_ps = (psum[:, 5], psum[:, 6, 0:384], psum[:, 7, 0:256], psum[:, 6, 384:512])

        def half(n):
            return slice(64 * n, 64 * n + 64)

        def tok(n):
            return slice(128 * n, 128 * n + 128)

        def tile_of(t, n):
            return t[:, bass.ds(n, 1)].rearrange("p a t -> p (a t)")

        def col(name, n=0):
            return par[:, bass.ds(COL[name] + n, 1)]

        @block.sync
        def _(sp):
            sp.dma_start(x[:], io["x"]).then_inc(sem("x_in"), 16)
            for t, name in ((par, "par"), (sel, "sel"), (ident, "ident"), (blk64, "blk64"), (idd, "idd")):
                sp.dma_start(t[:], io[name]).then_inc(sem("const_in"), 16)
            sp.dma_start(raw[:, 0], io["w"][0]).then_inc(sem("raw_in0"), 16)
            sp.dma_start(raw[:, 1], io["w"][1]).then_inc(sem("raw_in1"), 16)

            def load(i):
                for s in range(2):
                    sp.wait_ge(sem("lo_ready"), 2 * i + s + 1)
                    sp.dma_start(raw[:, s], io["w"][bass.ds(2 * i + s + 2, 1)].rearrange("a p n -> (a p) n"))\
                        .then_inc(sem(f"raw_in{s}"), 16)

            with sp.Fori(0, UNITS // 2 - 1) as i:
                load(i)
            sp.wait_ge(sem("x_added"), 24)
            sp.dma_start(io["y"], x[:]).then_inc(sem("stored"), 16)
            sp.wait_ge(sem("stored"), 16)

        @block.gpsimd
        def _(pool):
            def low_part(i):
                for s in range(2):
                    pool.wait_ge(sem("hi_ready"), 2 * i + s + 1)
                    pool.tensor_tensor(w_lo[:, s], raw[:, s], w_hi[:, s].bitcast(F32), ALU.subtract)\
                        .then_inc(sem("lo_ready"), 1)

            with pool.Fori(0, UNITS // 2) as i:
                low_part(i)

        @block.tensor
        def _(pe):
            def mm(out, lhsT, rhs, start=True, stop=True):
                return pe.matmul(out, lhsT, rhs, start=start, stop=stop)

            def mm3(out, slot, k, hi, lo, start, stop):
                a, b = w_hi[:, slot, tok(k)], w_lo[:, slot, tok(k)]
                mm(out, a, hi, start, False)
                mm(out, a, lo, False, False)
                return mm(out, b, hi, False, stop)

            def open_unit(g):
                pe.wait_ge(sem("lo_ready"), g.value(1))

            def open_bank(o):
                if o.at >= 2 or o.turn is not None:
                    pe.wait_ge(sem(f"freed{o.slot}"), o.half())

            def unit(g, o, hi, lo, ready=None, ks=range(8), start=0, stop=7):
                if ks[0] == 0:
                    open_unit(g)
                    if start == 0:
                        open_bank(o)
                for k in ks:
                    if ready:
                        pe.wait_ge(sem(ready[0]), ready[1] + k + 1)
                    last = mm3(psum[:, o.slot], g.slot, k, hi[:, k], lo[:, k], k == start, k == stop)
                if ks[-1] in (7, stop):
                    last.then_inc(sem("unit_used"), 1)

            def rms_stats(r, src):
                for k in range(KD):
                    pe.wait_ge(sem("squared"), KD * r + k + 1)
                    last = mm(p2, sel[:, 2:3].to_broadcast([128, 128]), src[:, k], k == 0, k == KD - 1)
                last.then_inc(sem("stat_sum"), 1)

            def spread_heads(bank, stat, c):
                for b in range(TB):
                    for h in range(2):
                        last = mm(bank[half(h), tok(b)],
                                  stat[:, c + 2 * b + h:c + 2 * b + h + 1].to_broadcast([128, 64]), ident[:])
                return last

            pe.wait_ge(sem("const_in"), 80)
            rms_stats(0, tmp)
            unit(Index(0), Index(0), h_hi, h_lo, ("h_ready", 0))
            with pe.Fori(0, A_UNITS // 2) as i:
                for c in (1, 2):
                    unit(Index(c, i, 2), Index(c, i, 2), h_hi, h_lo)

            pe.wait_ge(sem("cmp_in"), 48)
            pe.wait_ge(sem("blocks_ready"), 1)
            for c in range(2):
                for g in range(NG):
                    for l in range(32):
                        last = mm(p7[half(g), 32 * c:32 * c + NC], cmp_w1[half(g), c, l],
                                  blocks[half(g), c, l, 0:NC], l == 0, l == 31)
            last.then_inc(sem("cmp_mm"), 1)
            pe.wait_ge(sem("cmp_act"), 1)
            for g in range(NG):
                mm(p6[half(g), 0:NC], cmp_w2[half(g), 0], hid_cmp[half(g), 0, 0:NC])
            for g in range(NG):
                last = mm((p5, p4)[g][0:NC, 0:64], hid_cmp[half(g), 1, 0:NC], cmp_w2[half(g), 1])
            last.then_inc(sem("cmp_mm"), 1)
            pe.wait_ge(sem("cmp_act"), 2)
            mm(p6[:, 64:64 + NC], blk64[:], k_cmp[:, 1, 0:NC]).then_inc(sem("cmp_mm"), 1)
            pe.wait_ge(sem("qk_squared"), 1)
            for n in range(6):
                for b in range(TB):
                    last = mm(p2[:, 8 * n + 2 * b:8 * n + 2 * b + 2], tmp[:, n, tok(b)], sel[:, 0:2])
            last.then_inc(sem("qk_sum"), 1)
            for b in range(TB):
                pe.transpose(p3[:, tok(b)], u[:, 7, tok(b)], ident[:])
            for b in range(TB):
                pe.transpose(p4[:, tok(b)], u[:, 9, tok(b)], ident[:])
            for b in range(TB):
                last = pe.transpose(p7[:, tok(b)], u[:, 10, tok(b)], ident[:])
            last.then_inc(sem("nsa_tm"), 1)
            pe.wait_ge(sem("qk_rstd"), 1)
            pe.wait_ge(sem("cmp_keys"), 3)
            for n, bank in ((4, p5), (5, p6)):
                last = spread_heads(bank, rq, 8 * n)
            last.then_inc(sem("key_rstd"), 1)

            pe.wait_ge(sem("keys_ready"), 1)
            pe.wait_ge(sem("gates_ready"), 1)
            with pe.Fori(0, 4) as i:
                def pv(s):
                    b, g = s // 2, s % 2
                    pe.wait_ge(sem("pt_slc_ready"), 8 * i + s + 1)
                    pe.wait_ge(sem("pt_win_ready"), 8 * i + s + 1)
                    if g == 0:
                        pe.wait_ge(sem("nsa_out"), 4 * i + b)
                    out = p7[half(g), 0:128]
                    mm(out, v_cmp[0:NC, half(g)], pt_cmp[0:NC, :], True, False)
                    for n in range(b + 1):
                        mm(out, v_slc[:, n, half(g)], pt_slc[:, tok(n)], False, False)
                        last = mm(out, v_win[:, n, half(g)], pt_win[:, tok(n)], False, n == b)
                    last.then_inc(sem("pv_done"), 1)

                for s in range(8):
                    b, g = s // 2, s % 2
                    n = 128 * (b + 1)
                    if s == 0:
                        pe.wait_ge(sem("q_staged"), i + 1)
                    mm(p2[:, 0:n], q_st[half(g), tok(b)], u[half(g), 6, 0:n])
                    mm(p3[:, 0:n], q_st[half(g), tok(b)], u[half(g), 8, 0:n])
                    mm(p4[:, 0:NC], q_st[half(g), tok(b)], k_cmp[half(g), 0, 0:NC])\
                        .then_inc(sem("scores_ready"), 1)
                    if s:
                        pv(s - 1)
                    w = Index(A_UNITS + s // 2, i, 4)
                    unit(w, w, h_hi, h_lo, ks=range(0, 4) if s % 2 == 0 else range(4, 8))
                    pe.wait_ge(sem("probs_ready"), 8 * i + s + 1)
                    for m in range(b + 1):
                        pe.transpose(p5[:, tok(m)], s_slc[:, tok(m)], ident[:])
                    for m in range(b + 1):
                        pe.transpose(p6[:, tok(m)], s_win[:, tok(m)], ident[:])
                    pe.transpose(p7[0:NC, 256:384], s_cmp[:, 0:NC], ident[:])\
                        .then_inc(sem("probs_tm"), 1)
                pv(7)

            for c in range(16, 22):
                w = Index(A_UNITS + c)
                unit(w, w, h_hi, h_lo)
            pe.wait_ge(sem("lora_in"), 16)
            pe.wait_ge(sem("rank_ready"), 1)
            for c in range(4):
                if c:
                    pe.wait_ge(sem("lora_taken"), c)
                    pe.wait_ge(sem("lora_g_taken"), c)
                mm(p2, lora[0:64, 0, tok(c)], zm[0:64, 12, 0:T])
                mm(p3, lora[64:128, 0, tok(c)], zm[64:128, 12, 0:T])
                mm(p4, lora[:, 1, tok(c)], zm[:, 13, 0:T]).then_inc(sem("lora_done"), 1)

            with pe.Fori(0, 4) as i:
                pe.wait_ge(sem("kk_squared"), i + 1)
                for b in range(TB):
                    last = mm(p2[:, 2 * b:2 * b + 2], rk[:, tok(b)], sel[:, 0:2])
                last.then_inc(sem("kk_sum"), 1)
                w0 = Index(A_UNITS + 22, i, 2)
                w1 = Index(A_UNITS + 23, i, 2)
                unit(w0, w0, h_hi, h_lo)
                pe.wait_ge(sem("kk_rstd"), i + 1)
                pe.wait_ge(sem("rwkv_out"), i)
                last = spread_heads(p3, rs, 0)
                last.then_inc(sem("kk_bc"), 1)
                pe.wait_ge(sem("state_ready"), 9 * i + 1)
                def prepare_a(c, free):
                    pe.wait_ge(sem("y_taken"), 4 * i + free)
                    pe.wait_ge(sem("state_ready"), 9 * i + 2 * free + 1)
                    mm(p5[:, 0:128], ar[half(0), c, 0], bt[half(0), tok(c)]).then_inc(sem("d_half"), 1)
                    for q, src in enumerate((bt[:, tok(c)], ar[:, c, 0], kt[:, tok(c)], vt[:, tok(c)])):
                        last = pe.transpose(p2[:, tok(q)], src, ident[:])
                    last.then_inc(sem("tm_done"), 1)

                def prepare_b(c):
                    for h in range(2):
                        bank = (p3, p4)[h]
                        rhs = ar[half(h), c].rearrange("p a t -> p (a t)")
                        mm(bank[:, 0:256], bt[half(h), tok(c)], rhs)
                        mm(bank[:, 256:512], kt[half(h), tok(c)], rhs)
                    pe.wait_ge(sem("d_half"), 4 * i + c + 1)
                    mm(p5[:, 128:256], ar[half(1), c, 0], bt[half(1), tok(c)]).then_inc(sem("wkv_scores"), 1)

                def prepare_c(c):
                    pe.wait_ge(sem("sc_ready"), 4 * i + c + 1)
                    pe.wait_ge(sem("tm_ready"), 4 * i + c + 1)
                    for h in range(2):
                        last = mm(p5[:, 256 + 64 * h:320 + 64 * h], scs[c % 2][:, h, 256:384],
                                  tms[c % 2][:, 3, half(h)])
                    last.then_inc(sem("akv_done"), 1)

                prepare_a(0, 0)
                prepare_b(0)
                prepare_c(0)
                for c in range(4):
                    n = 4 * i + c
                    tm, sc, dm, wm = tms[c % 2], scs[c % 2], dms[c % 2], wms[c % 2]
                    pe.wait_ge(sem("wm_ready"), n + 1)
                    for lev in range(3):
                        dmat = dm if lev == 0 else (dd if lev == 1 else de)
                        if lev:
                            pe.wait_ge(sem("power_ready"), 5 * n + lev)
                        if lev < 2:
                            for h in range(2):
                                t_ = sc[:, h, 0:128] if lev == 0 else dmat[:, h, 1]
                                d_ = dm[:, h] if lev == 0 else dmat[:, h, 0]
                                mm(p7[:, 256 * h:256 * h + 128], t_, d_)
                                last = mm(p7[:, 256 * h + 128:256 * h + 256], d_, t_)
                            last.then_inc(sem("power_mm"), 1)
                        if lev:
                            pe.wait_ge(sem("solved"), 6 * n + lev)
                        for h in range(2):
                            t_ = sc[:, h, 0:128] if lev == 0 else dmat[:, h, 1]
                            last = mm(p6[:, 256 * h:256 * h + 256], t_, wm[:, h])
                        last.then_inc(sem("solve_mm"), 1)
                        if c < 3 and lev == 0:
                            prepare_a(c + 1, c)
                        if c < 3 and lev == 1:
                            prepare_b(c + 1)
                    pe.wait_ge(sem("solved"), 6 * n + 3)
                    for h in range(2):
                        last = pe.transpose(p7[:, 256 * h + 128:256 * h + 256], wm[:, h, 128:256], ident[:])
                    last.then_inc(sem("power_mm"), 1)
                    unit(w1, w1, h_hi, h_lo, ks=range(2 * c, 2 * c + 1))
                    for lev in range(3):
                        nmat = (dd, de, dd)[lev]
                        pe.wait_ge(sem("power_ready"), 5 * n + 3 + lev)
                        if lev < 2:
                            for h in range(2):
                                d_ = wm[:, h, 128:256] if lev == 0 else nmat[:, h, 0]
                                mm(p7[:, 256 * h:256 * h + 128], nmat[:, h, 1], d_)
                                last = mm(p7[:, 256 * h + 128:256 * h + 256], d_, nmat[:, h, 1])
                            last.then_inc(sem("power_mm"), 1)
                        if lev:
                            pe.wait_ge(sem("solved"), 6 * n + 3 + lev)
                        for h in range(2):
                            last = mm(p6[:, tok(h)], nmat[:, h, 1], wm[:, h, 0:128])
                        last.then_inc(sem("solve_mm"), 1)
                        if c < 3 and lev == 1:
                            prepare_c(c + 1)
                    pe.wait_ge(sem("solved"), 6 * n + 6)
                    if c < 3:
                        pe.wait_ge(sem("wm_ready"), n + 2)
                    for h in range(2):
                        mm(p2[half(h), 0:128], wm[:, h, 0:64], sc[:, h, 128:256])
                    for h in range(2):
                        for e in range(2):
                            bank = (p2, p5)[e]
                            mm(bank[half(h), 128:192], wm[half(e), h, 0:64], tm[half(e), 0, half(h)])
                            mm(bank[half(h), 192:256], tm[half(e), 0, half(h)], wm[half(e), h, 64:128], True, False)
                            last = mm(bank[half(h), 192:256], tm[half(e), 2, half(h)], tm[half(e), 3, half(h)],
                                      False, True)
                    last.then_inc(sem("pq_done"), 1)
                    unit(w1, w1, h_hi, h_lo, ks=range(2 * c + 1, 2 * c + 2))
                    pe.wait_ge(sem("pq_ready"), n + 1)
                    for h in range(2):
                        mm(p3[half(h), 0:128], wm[:, h, 64:128], sc[:, h, 128:256], True, False)
                    for e in range(2):
                        pe.wait_ge(sem("state_ready"), 9 * i + 2 * c + e + 1)
                        mm(p3[half(e), 0:128], tm[:, 3, half(e)], sc[:, e, 384:512], False, False)
                        for h in range(2):
                            last = mm(p3[half(h), half(e)], st[half(h), e], gt[half(h), half(e)], False, e == 1)
                        if e == 1:
                            last.then_inc(sem("y_done"), 1)
                        for h in range(2):
                            last = mm(p4[half(h), half(e)], pt[half(h), e], st[half(h), e])
                        last.then_inc(sem("state_mm"), 1)
                pe.wait_ge(sem("y_taken"), 4 * i + 4)
                mm(p2, blk64[:], bt).then_inc(sem("y_mean"), 1)
                pe.wait_ge(sem("state_ready"), 9 * i + 9)
                mm(p4, blk64[:], rk).then_inc(sem("bonus_mm"), 1)
                pe.wait_ge(sem("yc_squared"), i + 1)
                for b in range(TB):
                    last = mm(p5[:, 2 * b:2 * b + 2], kk[:, tok(b)], sel[:, 0:2])
                last.then_inc(sem("y_var"), 1)
                pe.wait_ge(sem("y_rstd"), i + 1)
                last = spread_heads(p3, rs, 8)
                last.then_inc(sem("y_bc"), 1)

            with pe.Fori(0, 4) as i:
                for c in range(2):
                    g = Index(FIRST["proj"] + c, i, 2)
                    open_unit(g)
                    open_bank(g)
                    pe.wait_ge(sem(f"freed_b{c}"), i)
                    for k in range(8):
                        pe.wait_ge(sem("h_ready"), 8 + k + 1)
                        bank = psum[:, g.slot] if k < 4 else psum[:, 2 + c]
                        last = mm3(bank, g.slot, k, h_hi[:, k], h_lo[:, k], k % 4 == 0, k % 4 == 3)
                    last.then_inc(sem("unit_used"), 1)
            with pe.Fori(0, 4) as i:
                for c in range(2):
                    g = Index(FIRST["out1"] + c, i, 2)
                    unit(g, g, y_hi, y_lo, ("y_ready", 0))

            def ffn_mm(f, hset, up, down, o):
                with pe.Fori(0, KF) as i:
                    for c in range(2):
                        unit(Index(FIRST[up] + c, i, 2), Index(o + c, i, 2), h_hi, h_lo, ("h_ready", 8 * hset))
                with pe.Fori(0, 4) as i:
                    for c in range(2):
                        for n in range(3):
                            unit(Index(FIRST[down] + 3 * c + n, i, 6), Index(o + 2 * KF + c, i, 2),
                                 hid_hi[:, 8 * n:], hid_lo[:, 8 * n:], ("hid_ready", KF * f + 8 * n),
                                 ks=range(8 if n < 2 else KF - 16),
                                 start=0 if n == 0 else -1, stop=KF - 17 if n == 2 else 99)

            rms_stats(1, tmp)
            ffn_mm(0, 2, "up1", "down1", 57)
            rms_stats(2, tmp)
            ffn_mm(1, 3, "up2", "down2", 109)
            rms_stats(3, sqz)
            rms_stats(4, tmp)

            pe.wait_ge(sem("consts2_in"), 96)
            with pe.Fori(0, 2) as i:
                for q in range(2):
                    hh = 2 * i + q
                    gu = Index(FIRST["mix"] + 11 * q, i, 22)
                    ou = Index(161 + 11 * q, i, 22)

                    def rotate(c):
                        slot = (161 + 11 * q + c) % 2
                        pe.wait_ge(sem(f"freed{slot}"), (ou + c).half() + 1)
                        pe.wait_ge(sem("roped"), 6 * hh + c)
                        mm(p2[0:32], rmat[:], qk_st[:, c]).then_inc(sem("rotated"), 1)

                    def v_blocks(n):
                        slot = (161 + 11 * q + 6 + n) % 2
                        pe.wait_ge(sem(f"freed{slot}"), (ou + 6 + n).half() + 1)
                        pe.wait_ge(sem("v_tm_ready"), 3 * hh + n)
                        if n == 0:
                            pe.wait_ge(sem("att_out"), 4 * hh)
                        for b in range(TB):
                            src = tmp[:, 4 + n, tok(b)] if n == 0 else tmp[:, 4 + n, b::4]
                            last = pe.transpose(p3[:, tok(b)], src, ident[:])
                        last.then_inc(sem("v_tm_done"), 1)

                    for c in range(9):
                        unit(gu + c, ou + c, h_hi, h_lo, ("h_ready", 32) if q == 0 else None)
                        if 1 <= c <= 6:
                            rotate(c - 1)
                        if c >= 7:
                            v_blocks(c - 7)
                    v_blocks(2)

                    def att_pv(r):
                        pe.wait_ge(sem("att_pt_a"), 4 * hh + r + 1)
                        pe.wait_ge(sem("att_pt_b"), 4 * hh + r + 1)
                        pe.wait_ge(sem("att_out"), 4 * hh + r)
                        for n in range(6):
                            v = v_tm[:, 0, n] if n < 4 else v_tm[:, n - 3, r]
                            last = mm(p3[:, 0:128], v, att_pT[:, tok(n)], n == 0, n == 5)
                        last.then_inc(sem("att_pv"), 1)

                    pe.wait_ge(sem("roped"), 6 * hh + 6)
                    pe.wait_ge(sem("v_tm_ready"), 3 * hh + 3)
                    for r in range(4):
                        mm(p4, qk_st[:, 0, r::4], qk_st[:, 3])
                        for n in (1, 2):
                            last = mm(p5[:, tok(n - 1)], qk_st[:, n, r::4], qk_st[:, 3 + n, r::4])
                        last.then_inc(sem("att_scores"), 1)
                        if r:
                            att_pv(r - 1)
                        c = 9 + r // 2
                        unit(gu + c, ou + c, h_hi, h_lo, ks=range(0, 4) if r % 2 == 0 else range(4, 8))
                        pe.wait_ge(sem("att_probs"), 4 * hh + r + 1)
                        for n in range(6):
                            last = pe.transpose((p6[:, tok(n)] if n < 4 else p7[:, tok(n - 4)]),
                                                att_p[:, tok(n)], ident[:])
                        last.then_inc(sem("att_tm"), 1)
                    att_pv(3)

            unit(Index(237), Index(205), h_hi, h_lo)
            pe.wait_ge(sem("row_a"), 4)
            with pe.Fori(0, 4) as i:
                gu, ou = Index(238, i, 10), Index(206, i, 10)

                def val_blocks(n):
                    slot = n % 2
                    pe.wait_ge(sem(f"freed{slot}"), (ou + 4 + n).half() + 1)
                    for b in range(TB):
                        last = pe.transpose((p2, p3)[n][:, tok(b)], tmp[:, 4 + n, tok(b)], ident[:])
                    last.then_inc(sem("ml_v_done"), 1)

                for c in range(8):
                    unit(gu + c, ou + c, h_hi, h_lo)
                    if c == 5:
                        pe.wait_ge(sem("ml_out"), 2 * i)
                        val_blocks(0)
                    if c == 6:
                        val_blocks(1)
                pe.wait_ge(sem("ml_v_ready"), 2 * i + 2)
                pe.wait_ge(sem("ml_q_ready"), 4 * i + 4)
                pe.wait_ge(sem("sel_staged"), i + 1)
                for b in range(TB):
                    out = ml_e_ps[b]
                    mm(out, c_row[0:4, tok(b)], selh[0:4, 0:T - 128 * b], True, False)
                    mm(out, selh[0:4, 0:128], nmu_row[0:4, 128 * b:T], False, False)
                    last = mm(out[:, 0:128], ident[:], mask_t[:], False, True)
                last.then_inc(sem("ml_exp_mm"), 1)
                for b in range(TB):
                    mm(ml_s_ps[b], ml_qk[:, 2, tok(b)], ml_qk[:, 0, 128 * b:T], True, False)
                    last = mm(ml_s_ps[b], ml_qk[:, 3, tok(b)], ml_qk[:, 1, 128 * b:T], False, True)
                last.then_inc(sem("ml_qk_mm"), 1)
                unit(gu + 8, ou + 8, h_hi, h_lo)
                pe.wait_ge(sem("ml_w_ready"), i + 1)
                for b in range(TB):
                    w = ml_w[:, ML_AT[b][0]:ML_AT[b][1]]
                    for n, lhsT in enumerate((ml_v[:, b, 0:128], ml_v[:, b, 128:256], ones128[:])):
                        last = mm(psum[:, 2 + n, 128 * b:T], lhsT, w, b == 0, b == TB - 1)
                mm(p5, selh[0:4, 0:128], em_row[0:4, :]).then_inc(sem("ml_num"), 1)
                unit(gu + 9, ou + 9, h_hi, h_lo)
                pe.wait_ge(sem("ml_squared"), i + 1)
                for b in range(TB):
                    for n in range(2):
                        last = mm(p6[:, b:b + 1], ml_sq[:, n, tok(b)], sel[:, 2:3], n == 0, n == 1)
                last.then_inc(sem("ml_sum"), 1)
                pe.wait_ge(sem("ml_rstd"), i + 1)
                for b in range(TB):
                    last = mm(p7[:, tok(b)], ml_small[:, 4 + b:5 + b].to_broadcast([128, 128]), ident[:])
                last.then_inc(sem("ml_bc"), 1)

            with pe.Fori(0, 2) as i:
                for j in range(2):
                    g = Index(FIRST["branch"] + 3 * j, i, 6)
                    open_unit(g)
                    for k in range(8):
                        c = k // 4
                        if k % 4 == 0:
                            pe.wait_ge(sem(f"freed_b{c}"), 2 * i + j + 4)
                        pe.wait_ge(sem("att_split"), k % 4 + 1)
                        last = mm3(psum[:, 2 + c], g.slot, k, ah_hi[:, k % 4], ah_lo[:, k % 4],
                                   k % 4 == 0, k % 4 == 3)
                    last.then_inc(sem("unit_used"), 1)
                    for c in range(2):
                        unit(g + 1 + c, Index(246 + 2 * j + c, i, 4), h_hi, h_lo, ("h_ready", 40))
            with pe.Fori(0, 4) as i:
                for c in range(2):
                    unit(Index(FIRST["out2"] + c, i, 2), Index(254 + c, i, 2), y2_hi, y2_lo, ("y_ready", 8))
            rms_stats(5, sqz)
            rms_stats(6, tmp)
            ffn_mm(2, 6, "up3", "down3", 262)
            rms_stats(7, sqz)

        @block.scalar
        def _(act):
            def high_part(g):
                act.wait_ge(sem(f"raw_in{g.slot}"), (g.half() + 1) * 16)
                if g.at >= 2 or g.turn is not None:
                    act.wait_ge(sem("unit_used"), g.value(-1))
                act.activation(w_hi[:, g.slot], raw[:, g.slot], ACT.Copy).then_inc(sem("hi_ready"), 1)

            def wait_apart(name, n, static):
                act.wait_ge(sem(name), n)
                act.wait_ge(sem(static), 16)

            def rms_act(r, src, dst, outputs=0, added=None):
                for k in range(KD):
                    done = outputs - KD + 1 + k
                    if done > 0:
                        act.wait_ge(sem("freed0"), (done + 1) // 2)
                        act.wait_ge(sem("freed1"), done // 2)
                    if added is not None:
                        act.wait_ge(sem("x_added"), added + k + 1)
                    act.activation(dst[:, k], src[:, k], ACT.Square).then_inc(sem("squared"), 1)
                act.wait_ge(sem("stat_sum"), r + 1)
                act.activation(p3, p2, ACT.Sqrt, bias=eps, scale=1.0 / D).then_inc(sem("stat_root"), 1)

            def round_h(nset, src):
                for k in range(KD):
                    act.wait_ge(sem("normed"), 8 * nset + k + 1)
                    act.activation(h_hi[:, k], src[:, k], ACT.Copy).then_inc(sem("rounded"), 1)

            act.wait_ge(sem("x_in"), 16)
            act.wait_ge(sem("const_in"), 80)
            high_part(Index(0))
            high_part(Index(1))
            rms_act(0, x, tmp)
            round_h(0, tmp)
            act.wait_ge(sem("h_ready"), 8)
            act.dma_start(cmp_w1, io["cmp_w1"]).then_inc(sem("cmp_in"), 16)
            act.dma_start(cmp_w2[:], io["cmp_w2"]).then_inc(sem("cmp_in"), 16)
            act.dma_start(cmp_pe[:], io["cmp_pe"]).then_inc(sem("cmp_in"), 16)
            act.dma_start(masks1[:], io["masks1"]).then_inc(sem("masks_in"), 16)
            high_part(Index(2))
            with act.Fori(0, A_UNITS // 2) as i:
                for c in (3, 4):
                    high_part(Index(c, i, 2))
            act.wait_ge(sem("cmp_mm"), 1)
            act.activation(hid_cmp[:, :, 0:NC], p7[:, 0:64].rearrange("p (c n) -> p c n", c=2)[:, :, 0:NC],
                           ACT.Silu).then_inc(sem("cmp_act"), 1)
            act.wait_ge(sem("cmp_keys"), 1)
            act.activation(k_cmp[:, 1, 0:NC], k_cmp[:, 0, 0:NC], ACT.Square).then_inc(sem("cmp_act"), 1)
            act.activation(tmp[:, 0:4], u[:, 0:4], ACT.Square)
            act.activation(tmp[:, 4], u[:, 6], ACT.Square)
            act.activation(tmp[:, 5], u[:, 8], ACT.Square).then_inc(sem("qk_squared"), 1)
            act.wait_ge(sem("cmp_mm"), 3)
            act.activation(k_cmp[:, 2, 0:NC], p6[:, 64:64 + NC], ACT.Sqrt, bias=eps, scale=1.0 / DH)\
                .then_inc(sem("cmp_act"), 1)
            act.wait_ge(sem("qk_sum"), 1)
            act.activation(rq[:], p2[:, 0:48], ACT.Sqrt, bias=eps, scale=1.0 / DH).then_inc(sem("qk_root"), 1)
            act.wait_ge(sem("nsa_tm"), 1)
            act.activation(v_win[:].rearrange("p b d -> p (b d)"), p4, ACT.Copy)
            act.activation(gate_tm[:], p7.rearrange("p (b n) -> p b n", b=TB)[:, :, 0:24], ACT.Sigmoid)\
                .then_inc(sem("gates_ready"), 1)
            with act.Fori(0, 4) as i:
                for s in range(8):
                    n = 128 * (s // 2 + 1)
                    act.wait_ge(sem("nb_ready"), 8 * i + s + 1)
                    for b, t_ in enumerate((s_cmp[:, 0:NC], s_slc[:, 0:n], s_win[:, 0:n])):
                        last = act.activation(t_, t_, ACT.Exp, bias=soft[:, 3 + b:4 + b],
                                              scale=q_scale[:, s:s + 1] if b else 1.0, accum_out=soft[:, 6 + b:7 + b])
                    last.then_inc(sem("exp_done"), 1)
                    act.wait_ge(sem("probs_tm"), 8 * i + s + 1)
                    act.activation(pt_slc[:, 0:n], p5[:, 0:n], ACT.Copy).then_inc(sem("pt_slc_ready"), 1)
                    if s % 2:
                        high_part(Index(A_UNITS + s // 2 + 2, i, 4))
            act.wait_ge(sem("omm_ready"), 1)
            for n in range(R_TILES):
                if n >= 8:
                    act.wait_ge(sem("mixed"), n - 7)
                act.activation(tmp[:, n % 8], zm[:, n, 1:], ACT.Copy, scale=omm[:, n:n + 1])\
                    .then_inc(sem("pre_mixed"), 1)
                if n in (1, 3):
                    high_part(Index(A_UNITS + 18 + n // 2))
            act.dma_start(lora[:], io["lora"]).then_inc(sem("lora_in"), 16)
            act.wait_ge(sem("mixed"), R_TILES)
            act.activation(zm[0:64, 12, 0:T], zm[0:64, 12, 0:T], ACT.Tanh)
            act.activation(zm[:, 13, 0:T], zm[:, 13, 0:T], ACT.Sigmoid).then_inc(sem("rank_ready"), 1)
            for c in range(20, 24):
                high_part(Index(A_UNITS + c))
            for c in range(4):
                act.wait_ge(sem("lora_done"), c + 1)
                act.activation(dw[:, c], p2, ACT.Sigmoid, bias=col("w0", c))
                act.activation(a_t[:, c], p3, ACT.Sigmoid, bias=col("a0", c)).then_inc(sem("lora_taken"), 1)
            act.wait_ge(sem("lora_taken"), 4)
            act.activation(dw[:], dw[:], ACT.Exp, scale=-DECAY).then_inc(sem("decay_ready"), 1)
            with act.Fori(0, 4) as i:
                act.wait_ge(sem("kk_made"), i + 1)
                act.activation(rk, kk, ACT.Square).then_inc(sem("kk_squared"), 1)
                wait_apart("kk_made", i + 1, "lora_in")
                act.activation(vt, tile_of(zm, 8 + i)[:, 0:T], ACT.Copy).then_inc(sem("v_staged"), 1)
                act.wait_ge(sem("kk_sum"), i + 1)
                act.activation(rs[:, 0:8], p2[:, 0:8], ACT.Sqrt).then_inc(sem("kk_root"), 1)
                high_part(Index(A_UNITS + 24, i, 2))
                def prepared(c):
                    tm, wm = tms[c % 2], wms[c % 2]
                    act.wait_ge(sem("tm_done"), 4 * i + c + 1)
                    act.activation(tm[:, 0], p2[:, 0:128], ACT.Copy, scale=-1.0)
                    act.activation(wm[:, :, 0:64], p2[:, 128:256].rearrange("p (h k) -> p h k", h=2), ACT.Copy)
                    act.activation(tm[:, 2:4].rearrange("p a n -> p (a n)"), p2[:, 256:512], ACT.Copy)\
                        .then_inc(sem("tm_ready"), 1)

                prepared(0)
                for c in range(4):
                    n = 4 * i + c
                    for lev in range(5):
                        act.wait_ge(sem("power_mm"), 5 * n + lev + 1)
                        dst = (dd, de, dd, de, dd)[lev]
                        if lev == 2:
                            act.activation(dst[:, :, 1], p7.rearrange("p (h a n) -> p h a n", h=2, a=2)[:, :, 1],
                                           ACT.Copy).then_inc(sem("power_ready"), 1)
                        else:
                            act.activation(dst[:].rearrange("p h a n -> p (h a n)"), p7, ACT.Copy)\
                                .then_inc(sem("power_ready"), 1)
                        if c < 3 and lev == 1:
                            prepared(c + 1)
                    act.wait_ge(sem("y_done"), n + 1)
                    act.activation(bt[:, tok(c)], p3[:, 0:128], ACT.Copy).then_inc(sem("y_taken"), 1)
                high_part(Index(A_UNITS + 25, i, 2))
                act.wait_ge(sem("yc_made"), i + 1)
                act.activation(kk, kt, ACT.Square).then_inc(sem("yc_squared"), 1)
                act.wait_ge(sem("y_var"), i + 1)
                act.activation(rs[:, 8:16], p5[:, 0:8], ACT.Sqrt, bias=lnx_eps, scale=1.0 / DH)\
                    .then_inc(sem("y_root"), 1)
            act.wait_ge(sem("rwkv_out"), 4)
            act.wait_ge(sem("unit_used"), 41)
            for k in range(KD):
                act.activation(h_hi[:, k], x[:, k], ACT.Copy).then_inc(sem("rounded"), 1)
            act.wait_ge(sem("freed0"), 21)
            act.wait_ge(sem("freed1"), 20)
            for n in range(4):
                v = zm[:, R_TILES + 4 * n:R_TILES + 4 * n + 4, 1:]
                act.activation(v, v, ACT.Sigmoid).then_inc(sem("merge_sig"), 1)
            act.wait_ge(sem("h_ready"), 16)
            act.dma_start(x[:], io["x"]).then_inc(sem("x_in"), 16)

            def round_y(yset, stage):
                with act.Fori(0, 4) as i:
                    for c in range(2):
                        wait_apart("merged", 8 * yset + 2 * i + c + 1, "lora_in")
                        act.activation(tile_of(y_hi, 2 * i + c), tmp[:, 2 * c], ACT.Copy)\
                            .then_inc(sem("y_rounded"), 1)
                        high_part(Index(FIRST[stage] + 2 + c, i, 2))

            def high_parts(first, count):
                with act.Fori(0, count // 2) as i:
                    for c in range(2):
                        high_part(Index(first + c, i, 2))

            round_y(0, "proj")
            high_parts(FIRST["out1"] + 2, 8)
            rms_act(1, x, tmp, 57)
            round_h(1, tmp)

            def ffn_act(f, up, down, o, last_down=24):
                with act.Fori(0, KF) as i:
                    if f == 0:
                        for c in range(2):
                            wait_apart("unit_used", Index(FIRST[up] + c, i, 2).value(1), "lora_in")
                            act.activation(tmp[:, c], psum[:, (o + c) % 2], ACT.Copy,
                                           scale=col("ffn_conv", 4 * KF + c + 2 * i)).then_inc(sem("scaled"), 1)
                            high_part(Index(FIRST[up] + 2 + c, i, 2))
                            if c == 0:
                                ob = Index(o, i, 2)
                                act.wait_ge(sem(f"freed{ob.slot}"), ob.half() + 1)
                                act.activation(tmp[:, 2], tmp[:, 0], ACT.Silu).then_inc(sem("silu_done"), 1)
                        wait_apart("gated", i + 1, "lora_in")
                    else:
                        gb, ub = Index(o, i, 2), Index(o + 1, i, 2)
                        wait_apart("unit_used", Index(FIRST[up], i, 2).value(1), "lora_in")
                        act.activation(tmp[:, 2], psum[:, gb.slot], ACT.Silu).then_inc(sem(f"freed{gb.slot}"), 1)
                        for c in range(2):
                            high_part(Index(FIRST[up] + 2 + c, i, 2))
                        wait_apart(f"freed{ub.slot}", ub.half() + 1, "lora_in")
                    act.activation(tile_of(hid_hi, i), tmp[:, 3], ACT.Copy).then_inc(sem("hid_rounded"), 1)
                high_parts(FIRST[down] + 2, last_down)

            ffn_act(0, "up1", "down1", 57)

            def post_act(r, outputs):
                rms_act(r, tmp, sqz, outputs)

            def pre_act(r, nset, added):
                rms_act(r, x, tmp, 0 if r > 2 else 109, added)
                round_h(nset, tmp)

            pre_act(2, 2, None)
            ffn_act(1, "up2", "down2", 109)
            post_act(3, 161)
            pre_act(4, 3, 0)
            act.dma_start(rope[:], io["rope"]).then_inc(sem("consts2_in"), 16)
            act.dma_start(rmat[:], io["rmat"]).then_inc(sem("consts2_in"), 16)
            act.dma_start(mask2[:], io["mask2"]).then_inc(sem("consts2_in"), 16)
            act.dma_start(mask_t[:], io["mask_t"]).then_inc(sem("consts2_in"), 16)
            act.dma_start(ones128[:], io["ones"]).then_inc(sem("consts2_in"), 16)
            act.dma_start(par_if[:], io["par_if"]).then_inc(sem("consts2_in"), 16)
            with act.Fori(0, 2) as i:
                for q in range(2):
                    hh = 2 * i + q
                    gu = Index(FIRST["mix"] + 11 * q + 2, i, 22)

                    def v_take(n):
                        act.wait_ge(sem("v_tm_done"), 3 * hh + n + 1)
                        act.activation(v_tm[:, n].rearrange("p b d -> p (b d)"), p3, ACT.Copy)\
                            .then_inc(sem("v_tm_ready"), 1)

                    for c in range(9):
                        high_part(gu + c)
                        if c == 8:
                            v_take(0)
                    v_take(1)
                    v_take(2)
                    for r in range(4):
                        act.wait_ge(sem("att_nb"), 4 * hh + r + 1)
                        act.activation(att_p[:], att_p[:], ACT.Exp, bias=att_small[:, 3:4], scale=128 ** -0.5,
                                       accum_out=att_small[:, 4:5]).then_inc(sem("att_exp"), 1)
                        act.wait_ge(sem("att_tm"), 4 * hh + r + 1)
                        act.activation(att_pT[:, 0:512], p6, ACT.Copy).then_inc(sem("att_pt_a"), 1)
                        if r % 2:
                            high_part(gu + 9 + r // 2)
            act.wait_ge(sem("att_out"), 16)
            act.dma_start(sel4[:], io["sel4"]).then_inc(sem("sel4_in"), 16)
            high_part(Index(239))
            act.wait_ge(sem("row_v"), 1)
            act.activation(rows[0:4, 1], rows[0:4, 0], ACT.Abs).then_inc(sem("row_a"), 1)
            act.wait_ge(sem("row_a"), 1)
            act.activation(rows[0:4, 1], rows[0:4, 1], ACT.Exp, scale=-1.0).then_inc(sem("row_a"), 1)
            act.wait_ge(sem("row_a"), 2)
            act.activation(rows[0:4, 1], rows[0:4, 1], ACT.Ln, bias=sel[0:4, 2:3]).then_inc(sem("row_a"), 1)
            act.wait_ge(sem("row_v"), 6)
            act.activation(em_row[0:4], em_row[0:4], ACT.Exp, scale=-1.0).then_inc(sem("row_a"), 1)
            with act.Fori(0, 4) as i:
                gu, ou = Index(238, i, 10), Index(206, i, 10)
                for c in range(8):
                    slot = c % 2
                    if c < 4:
                        wait_apart("unit_used", (gu + c).value(1), "lora_in")
                        t = 2 * i + (c if c < 2 else 6 + c)
                        act.activation(ml_qk[:, c], psum[:, slot], ACT.Identity, bias=col("conv_b", t),
                                       scale=col("conv_w", t + 48)).then_inc(sem("ml_scaled"), 1)
                        act.wait_ge(sem(f"freed{slot}"), (ou + c).half() + 1)
                        act.activation(ml_qk[:, c], ml_qk[:, c], ACT.Silu).then_inc(sem("ml_q_ready"), 1)
                    if c >= 6:
                        act.wait_ge(sem("unit_used"), (gu + c).value(1))
                        act.activation(ml_o[:, c - 6], psum[:, slot], ACT.Sigmoid).then_inc(sem(f"freed{slot}"), 1)
                    high_part(gu + c + 2)
                    if c in (6, 7):
                        n = c - 6
                        act.wait_ge(sem("ml_v_done"), 2 * i + n + 1)
                        act.activation(ml_v[:, :, tok(n)], (p2, p3)[n].rearrange("p (b d) -> p b d", b=TB),
                                       ACT.Copy).then_inc(sem("ml_v_ready"), 1)
                act.wait_ge(sem("ml_exp_mm"), i + 1)
                for b, (n0, n1) in enumerate(((0, 512), (512, 1024), (1024, 1280))):
                    last = act.activation(ml_e[:, n0:n1], psum[:, 2 + b, 0:n1 - n0], ACT.Exp)
                last.then_inc(sem("ml_exp"), 1)
                high_part(gu + 10)
                act.wait_ge(sem("ml_num"), i + 1)
                act.activation(ml_abs[:], p4, ACT.Abs).then_inc(sem("ml_abs_ready"), 1)
                high_part(gu + 11)
                act.wait_ge(sem("ml_h"), i + 1)
                act.activation(ml_sq[:], ml_hm[:], ACT.Square).then_inc(sem("ml_squared"), 1)
                act.wait_ge(sem("ml_sum"), i + 1)
                act.activation(ml_small[:, 0:4], p6[:, 0:4], ACT.Sqrt, bias=eps, scale=1.0 / 256)\
                    .then_inc(sem("ml_root"), 1)
            act.wait_ge(sem("ml_out"), 8)
            for k in range(4):
                act.activation(ah_hi[:, k], att_o[:, k], ACT.Copy).then_inc(sem("att_rounded"), 1)
            act.wait_ge(sem("unit_used"), FIRST["branch"])
            for k in range(KD):
                act.activation(h_hi[:, k], mo[:, k], ACT.Copy).then_inc(sem("rounded"), 1)
            for n in range(4):
                v = gates[:, 4 * n:4 * n + 4]
                act.activation(v, v, ACT.Sigmoid).then_inc(sem("merge_sig"), 1)
            with act.Fori(0, 2) as i:
                for j in range(2):
                    g = Index(FIRST["branch"] + 3 * j + 2, i, 6)
                    high_part(g)
                    for c in range(2):
                        high_part(g + 1 + c)
                        m = 4 * i + 2 * j + c
                        wait_apart("merged", m + 9, "lora_in")
                        act.activation(tile_of(y2_hi, m), tmp[:, 2 * c], ACT.Copy).then_inc(sem("y_rounded"), 1)
            high_parts(FIRST["out2"] + 2, 8)
            post_act(5, 262)
            pre_act(6, 4, 8)
            ffn_act(2, "up3", "down3", 262, 22)
            post_act(7, 314)

        @block.vector
        def _(dve):
            def take(g, o, dst):
                dve.wait_ge(sem("unit_used"), g.value(1))
                dve.tensor_scalar(dst, psum[:, o.slot], 1.0, None, ALU.mult).then_inc(sem(f"freed{o.slot}"), 1)

            def low_h(hset, k, src):
                dve.wait_ge(sem("rounded"), 8 * hset + k + 1)
                dve.tensor_tensor(h_lo[:, k], src[:, k], h_hi[:, k].bitcast(F32), ALU.subtract)\
                    .then_inc(sem("h_ready"), 1)

            def rms_rstd(r):
                dve.wait_ge(sem("stat_root"), r + 1)
                dve.reciprocal(p3, p3).then_inc(sem("stat_rstd"), 1)
                dve.wait_ge(sem("stat_rstd"), r + 1)

            def norm_h(r, hset, gains):
                rms_rstd(r)
                for k in range(KD):
                    dve.scalar_tensor_tensor(tmp[:, k], x[:, k], col(gains, k), p3, ALU.mult, ALU.mult)\
                        .then_inc(sem("normed"), 1)
                    if k:
                        low_h(hset, k - 1, tmp)
                low_h(hset, KD - 1, tmp)

            dve.memset(zm[:, 0:R_TILES, 0:1], 0.0).then_inc(sem("zero_col"), 1)
            dve.wait_ge(sem("x_in"), 16)
            dve.wait_ge(sem("const_in"), 80)
            norm_h(0, 0, "norm_mix")
            take(Index(0), Index(0), u[:, 0])
            with dve.Fori(0, A_UNITS // 2) as i:
                for c in (1, 2):
                    w = Index(c, i, 2)
                    take(w, w, tile_of(u, 2 * i + c))
            dve.wait_ge(sem("cmp_in"), 48)
            dve.wait_ge(sem("freed0"), 6)
            dve.wait_ge(sem("freed1"), 5)
            for c in range(2):
                src = u[:, 4 + c].rearrange("p (n s) -> p s n", s=16)
                for m in range(2):
                    last = dve.tensor_tensor(
                        blocks[:, c, 16 * m:16 * m + 16, 0:NC], src[:, :, m:m + NC],
                        cmp_pe[:, c, 16 * m:16 * m + 16].unsqueeze(2).to_broadcast([128, 16, NC]), ALU.add)
            last.then_inc(sem("blocks_ready"), 1)
            dve.tensor_scalar(gain[:, 0:3], par[:, COL["qk_gain"] + 1:COL["qk_gain"] + 4],
                              par[:, COL["qk_gain"]:COL["qk_gain"] + 1], None, ALU.mult).then_inc(sem("gain_ready"), 1)
            dve.wait_ge(sem("cmp_mm"), 2)
            dve.tensor_copy(v_cmp[0:NC, 0:64], p5[0:NC, 0:64])
            dve.tensor_copy(v_cmp[0:NC, 64:128], p4[0:NC, 0:64])
            dve.tensor_copy(k_cmp[:, 0, 0:NC], p6[:, 0:NC]).then_inc(sem("cmp_keys"), 1)
            dve.wait_ge(sem("cmp_act"), 3)
            dve.reciprocal(k_cmp[:, 2, 0:NC], k_cmp[:, 2, 0:NC]).then_inc(sem("cmp_keys"), 1)
            dve.wait_ge(sem("cmp_keys"), 2)
            dve.wait_ge(sem("gain_ready"), 1)
            dve.scalar_tensor_tensor(k_cmp[:, 0, 0:NC], k_cmp[:, 0, 0:NC], gain[:, 0:1], k_cmp[:, 2, 0:NC],
                                     ALU.mult, ALU.mult).then_inc(sem("cmp_keys"), 1)
            dve.wait_ge(sem("qk_root"), 1)
            dve.reciprocal(rq[:], rq[:]).then_inc(sem("qk_rstd"), 1)
            dve.wait_ge(sem("nsa_tm"), 1)
            dve.tensor_copy(v_slc[:].rearrange("p b d -> p (b d)"), p3)
            dve.wait_ge(sem("key_rstd"), 1)
            dve.scalar_tensor_tensor(u[:, 6], u[:, 6], gain[:, 1:2], p5, ALU.mult, ALU.mult)
            dve.scalar_tensor_tensor(u[:, 8], u[:, 8], gain[:, 2:3], p6, ALU.mult, ALU.mult)\
                .then_inc(sem("keys_ready"), 1)
            dve.wait_ge(sem("masks_in"), 16)
            dve.wait_ge(sem("gates_ready"), 1)
            dve.wait_ge(sem("qk_rstd"), 1)
            with dve.Fori(0, 4) as i:
                def output(s):
                    b = s // 2
                    dve.wait_ge(sem("pv_done"), 8 * i + s + 1)
                    dve.tensor_scalar(tile_of(o_nsa, i)[:, tok(b)], p7[:, 0:128], 1.0, None, ALU.mult)\
                        .then_inc(sem("nsa_out"), 1)

                dve.tensor_scalar(q_st[:], tile_of(u, i), 1.0, None, ALU.mult)
                dve.tensor_scalar(q_scale[:], rq[:, bass.ds(8 * i, 8)], DH ** -0.5, None, ALU.mult)
                for g in range(NG):
                    last = dve.tensor_scalar(gate_st[:, :, g], gate_tm[:, :, bass.ds(3 * i + 12 * g, 3)], 1.0, None,
                                             ALU.mult)
                last.then_inc(sem("q_staged"), 1)
                dve.wait_ge(sem("q_staged"), i + 1)
                for s in range(8):
                    b, g = s // 2, s % 2
                    n = 128 * (b + 1)
                    dve.wait_ge(sem("scores_ready"), 8 * i + s + 1)
                    dve.scalar_tensor_tensor(s_cmp[:, 0:NC], p4[:, 0:NC], q_scale[:, s:s + 1],
                                             cmp_add[:, b, 0:NC], ALU.mult, ALU.add)
                    for m, (dst, src) in enumerate(((s_slc[:, 0:n], p2[:, 0:n]), (s_win[:, 0:n], p3[:, 0:n]))):
                        last = dve.tensor_tensor_reduce(out=dst, in0=src, in1=causal[:, 384 - 128 * b:512],
                                                        scale=1.0, scalar=NEG, op0=ALU.add, op1=ALU.max,
                                                        accum_out=soft[:, 1 + m:2 + m])
                    last.then_inc(sem("maxes"), 1)
                    dve.wait_ge(sem("maxes"), 8 * i + s + 1)
                    dve.tensor_reduce(soft[:, 3:4], s_cmp[:, 0:NC], AX.X, ALU.max, negate=True)
                    dve.tensor_scalar(soft[:, 4:6], soft[:, 1:3], q_scale[:, s:s + 1], -1.0, ALU.mult, ALU.mult)\
                        .then_inc(sem("nb_ready"), 1)
                    if s and g == 0:
                        output(s - 1)
                    dve.wait_ge(sem("exp_done"), 8 * i + s + 1)
                    dve.reciprocal(soft[:, 12:15], soft[:, 6:9]).then_inc(sem("sum_inv"), 1)
                    dve.wait_ge(sem("sum_inv"), 8 * i + s + 1)
                    dve.tensor_tensor(soft[:, 9:12], soft[:, 12:15], gate_st[:, b, g], ALU.mult)\
                        .then_inc(sem("coef"), 1)
                    dve.wait_ge(sem("coef"), 8 * i + s + 1)
                    dve.scalar_tensor_tensor(s_cmp[:, 0:NC], s_cmp[:, 0:NC], soft[:, 9:10], cmp_mul[:, b, 0:NC],
                                             ALU.mult, ALU.mult)
                    dve.tensor_scalar(s_slc[:, 0:n], s_slc[:, 0:n], soft[:, 10:11], None, ALU.mult)
                    dve.tensor_scalar(s_win[:, 0:n], s_win[:, 0:n], soft[:, 11:12], None, ALU.mult)\
                        .then_inc(sem("probs_ready"), 1)
                    dve.wait_ge(sem("probs_tm"), 8 * i + s + 1)
                    dve.tensor_copy(pt_cmp[0:NC], p7[0:NC, 256:384])
                    dve.tensor_copy(pt_win[:, 0:n], p6[:, 0:n]).then_inc(sem("pt_win_ready"), 1)
                    if g:
                        w = Index(A_UNITS + b, i, 4)
                        take(w, w, tile_of(zm, 4 * i + b)[:, 1:])
                output(7)
            dve.tensor_scalar(omm[:, 0:14], par[:, COL["mu"]:COL["mu"] + 14], -1.0, 1.0, ALU.mult, ALU.add)
            dve.tensor_scalar(omm[:, 14:18], par[:, COL["k_a"]:COL["k_a"] + 4], -1.0, 1.0, ALU.mult, ALU.add)\
                .then_inc(sem("omm_ready"), 1)
            dve.wait_ge(sem("zero_col"), 1)
            dve.wait_ge(sem("freed0"), 14)
            dve.wait_ge(sem("freed1"), 13)
            for n in range(R_TILES):
                dve.wait_ge(sem("pre_mixed"), n + 1)
                dve.scalar_tensor_tensor(zm[:, n, 0:T], zm[:, n, 0:T], col("mu", n), tmp[:, n % 8],
                                         ALU.mult, ALU.add).then_inc(sem("mixed"), 1)
            for c in range(16, 22):
                w = Index(A_UNITS + c)
                take(w, w, zm[:, c, 1:])
            for c in range(4):
                dve.wait_ge(sem("lora_done"), c + 1)
                dve.tensor_copy(g_t[:, c], p4).then_inc(sem("lora_g_taken"), 1)
            dve.wait_ge(sem("decay_ready"), 1)
            dve.wait_ge(sem("mixed"), R_TILES)
            dve.wait_ge(sem("omm_ready"), 1)
            with dve.Fori(0, 4) as i:
                chain = [0]

                def link(ins, per=PREP):
                    chain[0] += 1
                    ins.then_inc(sem("prep"), 1)
                    dve.wait_ge(sem("prep"), per * i + chain[0])

                def zt(n):
                    return tile_of(zm, n + i)[:, 0:T]

                def pairs(t):
                    return t.rearrange("p (c e n) -> p c e n", c=4, e=2)

                dwt = tile_of(dw, i)
                dve.tensor_scalar(kk, zt(4), col("k_k", i), None, ALU.mult).then_inc(sem("kk_made"), 1)
                dve.wait_ge(sem("rwkv_out"), i)
                link(dve.memset(kt, 0.0))
                link(dve.tensor_scalar(kt[:, ::64], dwt[:, ::64], 1.0, None, ALU.mult))
                link(dve.tensor_scalar(dwt[:, ::64], dwt[:, ::64], 0.0, None, ALU.mult))
                link(dve.tensor_tensor_scan(l_t, dwt, kt, 0.0, ALU.mult, ALU.add))
                link(dve.reciprocal(li, l_t))
                dve.tensor_tensor(ar[:, :, 1], zt(0).rearrange("p (c n) -> p c n", c=4),
                                  l_t.rearrange("p (c n) -> p c n", c=4), ALU.mult)
                link(dve.tensor_scalar(kh, tile_of(a_t, i), col("k_a", i), omm[:, bass.ds(14 + i, 1)],
                                       ALU.mult, ALU.add))
                link(dve.tensor_tensor(kh, kh, zt(4), ALU.mult))
                link(dve.tensor_tensor(kt, kh, li, ALU.mult))
                dve.wait_ge(sem("kk_root"), i + 1)
                link(dve.tensor_scalar(rs[:, 0:8], rs[:, 0:8], 1e-12, None, ALU.max))
                dve.reciprocal(rs[:, 0:8], rs[:, 0:8]).then_inc(sem("kk_rstd"), 1)
                dve.wait_ge(sem("kk_bc"), i + 1)
                link(dve.tensor_tensor(kk, kk, p3, ALU.mult))
                dve.tensor_tensor(ar[:, :, 0].rearrange("p c (e n) -> p c e n", e=2)[:, :, :, 1:],
                                  pairs(kk)[:, :, :, 1:], pairs(l_t)[:, :, :, 0:63], ALU.mult)
                dve.tensor_copy(ar[:, :, 0].rearrange("p c (e n) -> p c e n", e=2)[:, :, :, 0], pairs(kk)[:, :, :, 0])
                link(dve.tensor_tensor(bt, kk, tile_of(a_t, i), ALU.mult))
                link(dve.tensor_tensor(bt, bt, li, ALU.mult))
                dve.scalar_tensor_tensor(rk, zt(0), col("r_k", i), kh, ALU.mult, ALU.mult)
                dve.wait_ge(sem("v_staged"), i + 1)
                assert chain[0] == PREP
                dve.memset(st[:, 0], 0.0).then_inc(sem("state_ready"), 1)
                w = Index(A_UNITS + 22, i, 2)
                take(w, w, tile_of(zm, 22 + 2 * i)[:, 1:])
                def masked_a(c):
                    sc = scs[c % 2]
                    dve.wait_ge(sem("wkv_scores"), 4 * i + c + 1)
                    dve.tensor_tensor(sc[:, 0], p3, pair_mask, ALU.mult)
                    dve.tensor_tensor(sc[:, 1], p4, pair_mask, ALU.mult)

                def masked_b(c):
                    dm, wm = dms[c % 2], wms[c % 2]
                    for h in range(2):
                        dve.tensor_tensor(dm[:, h], p5[:, tok(h)], sub_mask[:, 0], ALU.mult)
                        last = dve.tensor_tensor(wm[:, h, 128:256], p5[:, tok(h)], sub_mask[:, 1], ALU.mult)
                    last.then_inc(sem("sc_ready"), 1)

                def masked_c(c):
                    dve.wait_ge(sem("tm_ready"), 4 * i + c + 1)
                    dve.wait_ge(sem("akv_done"), 4 * i + c + 1)
                    dve.tensor_copy(wms[c % 2][:, :, 64:128], p5[:, 256:384].rearrange("p (h v) -> p h v", h=2))\
                        .then_inc(sem("wm_ready"), 1)

                masked_a(0)
                masked_b(0)
                masked_c(0)
                for c in range(4):
                    n = 4 * i + c
                    wm = wms[c % 2]
                    dve.wait_ge(sem("wm_ready"), n + 1)
                    for lev in range(6):
                        m = 256 if lev < 3 else 128
                        dve.wait_ge(sem("solve_mm"), 6 * n + lev + 1)
                        dve.tensor_tensor(wm[:, :, 0:m], wm[:, :, 0:m],
                                          p6[:, 0:2 * m].rearrange("p (h n) -> p h n", h=2), ALU.add)\
                            .then_inc(sem("solved"), 1)
                        if c < 3 and lev in (2, 3, 5):
                            (masked_a, masked_b, None, masked_c)[lev - 2](c + 1)
                    dve.wait_ge(sem("pq_done"), n + 1)
                    dve.tensor_tensor(gt[:], p2[:, 0:128], ar[:, c, 1], ALU.add)
                    for e in range(2):
                        end = 128 * c + 64 * e + 63
                        dve.tensor_tensor(pt[:, e], (p2, p5)[e][:, 128:192], idd[:], ALU.add)
                        last = dve.tensor_scalar(ql[:, e], (p2, p5)[e][:, 192:256], l_t[:, end:end + 1],
                                                 None, ALU.mult)
                    last.then_inc(sem("pq_ready"), 1)
                    dve.wait_ge(sem("pq_ready"), n + 1)
                    for e in range(2):
                        end = 128 * c + 64 * e + 63
                        dve.wait_ge(sem("state_mm"), 8 * i + 2 * c + e + 1)
                        dve.scalar_tensor_tensor(st[:, 1 - e], p4[:, half(e)], l_t[:, end:end + 1], ql[:, e],
                                                 ALU.mult, ALU.add).then_inc(sem("state_ready"), 1)
                w = Index(A_UNITS + 23, i, 2)
                take(w, w, tile_of(zm, 23 + 2 * i)[:, 1:])
                dve.wait_ge(sem("y_mean"), i + 1)
                dve.scalar_tensor_tensor(kt, p2, -1.0 / DH, bt, ALU.mult, ALU.add).then_inc(sem("yc_made"), 1)
                dve.wait_ge(sem("bonus_mm"), i + 1)
                dve.tensor_tensor(kh, p4, vt, ALU.mult)
                dve.wait_ge(sem("y_root"), i + 1)
                dve.reciprocal(rs[:, 8:16], rs[:, 8:16]).then_inc(sem("y_rstd"), 1)
                dve.wait_ge(sem("y_bc"), i + 1)
                dve.scalar_tensor_tensor(kt, kt, col("ln_w", i), p3, ALU.mult, ALU.mult).then_inc(sem("post"), 1)
                dve.wait_ge(sem("post"), 2 * i + 1)
                dve.scalar_tensor_tensor(kt, kt, col("ln_b", i), kh, ALU.add, ALU.add).then_inc(sem("post"), 1)
                dve.wait_ge(sem("post"), 2 * i + 2)
                dve.tensor_tensor(tile_of(o_rwkv, i), kt, tile_of(g_t, i), ALU.mult).then_inc(sem("rwkv_out"), 1)
            for k in range(KD):
                low_h(1, k, x)
            dve.wait_ge(sem("merge_sig"), 4)

            def low_y(yset, i, c):
                dve.wait_ge(sem("y_rounded"), 8 * yset + 2 * i + c + 1)
                dve.tensor_tensor(tile_of(y_lo, 2 * i + c), tmp[:, 2 * c], tile_of(y_hi, 2 * i + c).bitcast(F32),
                                  ALU.subtract).then_inc(sem("y_ready"), 1)

            with dve.Fori(0, 4) as i:
                for c in range(2):
                    g = Index(FIRST["proj"] + c, i, 2)
                    dve.wait_ge(sem("unit_used"), g.value(1))
                    dve.tensor_tensor(tmp[:, 2 * c], psum[:, g.slot], tile_of(zm, R_TILES + 2 * i + c)[:, 1:],
                                      ALU.mult).then_inc(sem(f"freed{g.slot}"), 1)
                    dve.tensor_tensor(tmp[:, 2 * c + 1], psum[:, 2 + c], tile_of(zm, R_TILES + 8 + 2 * i + c)[:, 1:],
                                      ALU.mult).then_inc(sem(f"freed_b{c}"), 1)
                    dve.wait_ge(sem(f"freed_b{c}"), i + 1)
                    dve.tensor_tensor(tmp[:, 2 * c], tmp[:, 2 * c], tmp[:, 2 * c + 1], ALU.add)\
                        .then_inc(sem("merged"), 1)
                    low_y(0, i, c)

            def add_to_x(stage, o, per_unit=1):
                with dve.Fori(0, 4) as i:
                    for c in range(2):
                        ob = Index(o + c, i, 2)
                        dve.wait_ge(sem("unit_used"),
                                    Index(FIRST[stage] + per_unit * (c + 1) - 1, i, 2 * per_unit).value(1))
                        xt = tile_of(x, 2 * i + c)
                        dve.tensor_tensor(xt, xt, psum[:, ob.slot], ALU.add).then_inc(sem(f"freed{ob.slot}"), 1)

            dve.wait_ge(sem("x_in"), 32)
            add_to_x("out1", 49)

            def ffn_dve(f, up, o):
                with dve.Fori(0, KF) as i:
                    for c in range(2):
                        slot = (o + c) % 2
                        if f == 0:
                            dve.wait_ge(sem("scaled"), 2 * i + c + 1)
                            dve.scalar_tensor_tensor(tmp[:, c, 1:], psum[:, slot, 0:T - 1],
                                                     col("ffn_conv", 2 * KF + c + 2 * i), tmp[:, c, 1:],
                                                     ALU.mult, ALU.add).then_inc(sem("conv_half"), 1)
                            dve.wait_ge(sem("conv_half"), 2 * i + c + 1)
                            dve.scalar_tensor_tensor(tmp[:, c, 2:], psum[:, slot, 0:T - 2],
                                                     col("ffn_conv", c + 2 * i), tmp[:, c, 2:],
                                                     ALU.mult, ALU.add)\
                                .then_inc(sem(f"freed{slot}"), 1)
                    ub = Index(o + 1, i, 2)
                    if f == 0:
                        dve.wait_ge(sem("silu_done"), i + 1)
                        dve.wait_ge(sem(f"freed{ub.slot}"), ub.half() + 1)
                        dve.tensor_tensor(tmp[:, 3], tmp[:, 2], tmp[:, 1], ALU.mult).then_inc(sem("gated"), 1)
                    else:
                        gb = Index(o, i, 2)
                        dve.wait_ge(sem(f"freed{gb.slot}"), gb.half() + 1)
                        dve.wait_ge(sem("hid_ready"), KF * f + i)
                        dve.wait_ge(sem("unit_used"), Index(FIRST[up] + 1, i, 2).value(1))
                        dve.tensor_tensor(tmp[:, 3], tmp[:, 2], psum[:, ub.slot], ALU.mult)\
                            .then_inc(sem(f"freed{ub.slot}"), 1)
                    dve.wait_ge(sem("hid_rounded"), KF * f + i + 1)
                    dve.tensor_tensor(tile_of(hid_lo, i), tmp[:, 3], tile_of(hid_hi, i).bitcast(F32), ALU.subtract)\
                        .then_inc(sem("hid_ready"), 1)

            norm_h(1, 2, "norm_ffn")
            ffn_dve(0, "up1", 57)
            add_to_x("down1", 57 + 2 * KF, 3)

            def f_tiles(stage, o, per_unit):
                with dve.Fori(0, 4) as i:
                    for c in range(2):
                        take(Index(FIRST[stage] + per_unit * (c + 1) - 1, i, 2 * per_unit),
                             Index(o + c, i, 2), tile_of(tmp, 2 * i + c))

            def post_norm(r, gains, factor):
                rms_rstd(r)
                n = (r - 3) // 2 * 8
                for k in range(KD + 1):
                    if k < KD:
                        dve.scalar_tensor_tensor(sqz[:, k], tmp[:, k], col(gains, k), p3, ALU.mult, ALU.mult)\
                            .then_inc(sem("post_scaled"), 1)
                    if k:
                        dve.wait_ge(sem("post_scaled"), n + k)
                        dve.scalar_tensor_tensor(x[:, k - 1], sqz[:, k - 1], factor, x[:, k - 1],
                                                 ALU.mult, ALU.add).then_inc(sem("x_added"), 1)

            norm_h(2, 3, "ffn1_pre")
            ffn_dve(1, "up2", 109)
            f_tiles("down2", 153, 3)
            post_norm(3, "ffn1_post", 0.5)
            norm_h(4, 4, "mix_pre")
            dve.wait_ge(sem("consts2_in"), 96)
            with dve.Fori(0, 2) as i:
                for q in range(2):
                    hh = 2 * i + q
                    gu = Index(FIRST["mix"] + 11 * q, i, 22)
                    ou = Index(161 + 11 * q, i, 22)

                    def rope_it(c):
                        dve.wait_ge(sem(f"freed{(ou + c).slot}"), (ou + c).half() + 1)
                        dve.tensor_tensor(qk_st[0:32, c], qk_st[0:32, c], rope[:, 0], ALU.mult)
                        dve.tensor_tensor(rope_t[:], p2[0:32], rope[:, 1], ALU.mult).then_inc(sem("rope_a"), 1)
                        dve.wait_ge(sem("rope_a"), 6 * hh + c + 1)
                        dve.tensor_tensor(qk_st[0:32, c], qk_st[0:32, c], rope_t[:], ALU.add)\
                            .then_inc(sem("roped"), 1)

                    for c in range(9):
                        take(gu + c, ou + c, qk_st[:, c] if c < 6 else tmp[:, c - 2])
                        if 1 <= c <= 6:
                            dve.wait_ge(sem("rotated"), 6 * hh + c)
                            rope_it(c - 1)

                    def att_output(r):
                        dve.wait_ge(sem("att_pv"), 4 * hh + r + 1)
                        dve.tensor_scalar(tile_of(att_o, hh)[:, r::4], p3[:, 0:128], 1.0, None, ALU.mult)\
                            .then_inc(sem("att_out"), 1)

                    for r in range(4):
                        n = 4 * hh + r + 1
                        dve.wait_ge(sem("att_scores"), n)
                        dve.memset(att_small[:, 6:7], 0.0)
                        dve.tensor_tensor_reduce(out=att_p[:, 0:512], in0=p4, in1=mask2[:, r, 0:512], scale=1.0,
                                                 scalar=NEG, op0=ALU.add, op1=ALU.max, accum_out=att_small[:, 0:1])
                        dve.tensor_tensor_reduce(out=att_p[:, 512:768], in0=p5[:, 0:256], in1=mask2[:, r, 512:768],
                                                 scale=1.0, scalar=NEG, op0=ALU.add, op1=ALU.max,
                                                 accum_out=att_small[:, 1:2]).then_inc(sem("att_max"), 1)
                        dve.wait_ge(sem("att_max"), n)
                        dve.tensor_scalar(att_small[:, 3:4], att_small[:, 0:1], att_small[:, 1:2], -(128 ** -0.5),
                                          ALU.max, ALU.mult).then_inc(sem("att_nb"), 1)
                        if r:
                            att_output(r - 1)
                        dve.wait_ge(sem("att_exp"), n)
                        dve.reciprocal(att_small[:, 5:6], att_small[:, 4:5]).then_inc(sem("att_inv"), 1)
                        dve.wait_ge(sem("att_inv"), n)
                        dve.tensor_scalar(att_p[:], att_p[:], att_small[:, 5:6], None, ALU.mult)\
                            .then_inc(sem("att_probs"), 1)
                        dve.wait_ge(sem("att_tm"), n)
                        dve.tensor_copy(att_pT[:, 512:768], p7[:, 0:256]).then_inc(sem("att_pt_b"), 1)
                        if r % 2:
                            c = 9 + r // 2
                            take(gu + c, ou + c, tile_of(gates, 2 * hh + r // 2))
                    att_output(3)
            dve.wait_ge(sem("unit_used"), 238)
            dve.memset(zero_row, 0.0)
            dve.wait_ge(sem("sel4_in"), 16)
            dve.tensor_scalar(rows[0:4, 0], psum[32:36, 1], par_if[0:4, 1:2], None, ALU.add).then_inc(sem("row_v"), 1)
            dve.tensor_scalar(rows[0:4, 2], psum[0:4, 1], par_if[0:4, 0:1], None, ALU.add).then_inc(sem("freed1"), 1)
            dve.wait_ge(sem("row_a"), 3)
            dve.scalar_tensor_tensor(rows[0:4, 3], rows[0:4, 0], 0.0, rows[0:4, 1], ALU.min, ALU.subtract)\
                .then_inc(sem("row_v"), 1)
            dve.wait_ge(sem("row_v"), 2)
            dve.tensor_tensor_scan(b_row, rows[0:4, 3], zero_row, 0.0, ALU.add, ALU.add)\
                .then_inc(sem("row_v"), 1)
            dve.wait_ge(sem("row_v"), 3)
            dve.tensor_tensor(c_row[0:4], rows[0:4, 2], b_row, ALU.subtract).then_inc(sem("row_v"), 1)
            dve.wait_ge(sem("row_v"), 4)
            dve.tensor_tensor_scan(nmu_row[0:4], c_row[0:4], zero_row, 0.0, ALU.max, ALU.max)\
                .then_inc(sem("row_v"), 1)
            dve.wait_ge(sem("row_v"), 5)
            dve.tensor_tensor(em_row[0:4], b_row, nmu_row[0:4], ALU.add).then_inc(sem("row_v"), 1)
            dve.wait_ge(sem("row_v"), 6)
            dve.tensor_scalar(nmu_row[0:4], nmu_row[0:4], -1.0, None, ALU.mult)
            with dve.Fori(0, 4) as i:
                gu, ou = Index(238, i, 10), Index(206, i, 10)
                dve.tensor_scalar(selh[0:4], sel4[0:4, bass.ds(i, 1)].rearrange("p a t -> p (a t)"), 1.0, None,
                                  ALU.mult).then_inc(sem("sel_staged"), 1)
                for c in range(4):
                    slot = c % 2
                    t = 2 * i + (c if c < 2 else 6 + c)
                    dve.wait_ge(sem("ml_scaled"), 4 * i + c + 1)
                    for n in (1, 2, 3):
                        ins = dve.scalar_tensor_tensor(ml_qk[:, c, n:], psum[:, slot, 0:T - n],
                                                       col("conv_w", t + 48 - 16 * n), ml_qk[:, c, n:],
                                                       ALU.mult, ALU.add)
                        if n < 3:
                            ins.then_inc(sem("ml_conv"), 1)
                            dve.wait_ge(sem("ml_conv"), 8 * i + 2 * c + n)
                        else:
                            ins.then_inc(sem(f"freed{slot}"), 1)
                for c in (4, 5):
                    take(gu + c, ou + c, tmp[:, c])
                dve.wait_ge(sem("ml_exp"), i + 1)
                dve.wait_ge(sem("ml_qk_mm"), i + 1)
                for b, (n0, n1) in enumerate(((0, 512), (512, 1024), (1024, 1280))):
                    last = dve.scalar_tensor_tensor(ml_w[:, n0:n1], psum[:, 5 + b, 0:n1 - n0], 1.0 / 16,
                                                    ml_e[:, n0:n1], ALU.mult, ALU.mult)
                last.then_inc(sem("ml_w_ready"), 1)
                take(gu + 8, ou + 8, tile_of(gates, 8 + 2 * i))
                dve.wait_ge(sem("ml_abs_ready"), i + 1)
                dve.tensor_tensor(ml_d[:], p5, ml_abs[:], ALU.max).then_inc(sem("ml_den"), 1)
                dve.wait_ge(sem("ml_den"), 2 * i + 1)
                dve.reciprocal(ml_d[:], ml_d[:]).then_inc(sem("ml_den"), 1)
                dve.wait_ge(sem("ml_den"), 2 * i + 2)
                dve.tensor_tensor(ml_hm[:, 0], p2, ml_d[:], ALU.mult)
                dve.tensor_tensor(ml_hm[:, 1], p3, ml_d[:], ALU.mult).then_inc(sem("ml_h"), 1)
                take(gu + 9, ou + 9, tile_of(gates, 9 + 2 * i))
                dve.wait_ge(sem("ml_root"), i + 1)
                dve.reciprocal(ml_small[:, 4:8], ml_small[:, 0:4]).then_inc(sem("ml_rstd"), 1)
                dve.wait_ge(sem("ml_bc"), i + 1)
                for n in range(2):
                    dve.scalar_tensor_tensor(ml_hm[:, n], ml_hm[:, n], col("head_g", 2 * i + n), p7,
                                             ALU.mult, ALU.mult).then_inc(sem("ml_normed"), 1)
                for n in range(2):
                    dve.wait_ge(sem("ml_normed"), 2 * i + n + 1)
                    dve.tensor_tensor(tile_of(mo, 2 * i + n), ml_hm[:, n], ml_o[:, n], ALU.mult)\
                        .then_inc(sem("ml_out"), 1)
            for k in range(4):
                dve.wait_ge(sem("att_rounded"), k + 1)
                dve.tensor_tensor(ah_lo[:, k], att_o[:, k], ah_hi[:, k].bitcast(F32), ALU.subtract)\
                    .then_inc(sem("att_split"), 1)
            for k in range(KD):
                low_h(5, k, mo)
            dve.wait_ge(sem("merge_sig"), 8)
            with dve.Fori(0, 2) as i:
                for j in range(2):
                    for c in range(2):
                        m = 4 * i + 2 * j + c
                        g = Index(FIRST["branch"] + 3 * j + 1 + c, i, 6)
                        ob = Index(246 + 2 * j + c, i, 4)
                        dve.wait_ge(sem("unit_used"), g.value(1))
                        dve.tensor_tensor(tmp[:, 2 * c], psum[:, ob.slot], tile_of(gates, 8 + m), ALU.mult)\
                            .then_inc(sem(f"freed{ob.slot}"), 1)
                        dve.tensor_tensor(tmp[:, 2 * c + 1], psum[:, 2 + c], tile_of(gates, m), ALU.mult)\
                            .then_inc(sem(f"freed_b{c}"), 1)
                        dve.wait_ge(sem(f"freed_b{c}"), 2 * i + j + 5)
                        dve.tensor_tensor(tmp[:, 2 * c], tmp[:, 2 * c], tmp[:, 2 * c + 1], ALU.add)\
                            .then_inc(sem("merged"), 1)
                        dve.wait_ge(sem("y_rounded"), m + 9)
                        dve.tensor_tensor(tile_of(y2_lo, m), tmp[:, 2 * c], tile_of(y2_hi, m).bitcast(F32),
                                          ALU.subtract).then_inc(sem("y_ready"), 1)
            f_tiles("out2", 254, 1)
            post_norm(5, "mix_post", 1.0)
            norm_h(6, 6, "ffn2_pre")
            ffn_dve(2, "up3", 262)
            f_tiles("down3", 306, 3)
            post_norm(7, "ffn2_post", 0.5)




def _shape_constants():
    p = np.arange(128)
    i512 = np.arange(512)
    f = np.float32
    causal = np.where(i512[None, :] <= p[:, None] + 384, 0, NEG)
    t = 128 * np.arange(4)[None, :, None] + p[:, None, None]
    n = np.arange(32)[None, None, :]
    ok = (16 * n + 31 <= t) & (n < NC)
    cmp_add = np.where(ok, 0, NEG).reshape(128, 128)
    cmp_mul = ok.reshape(128, 128)
    row, colm = p[:, None], p[None, :]
    chunk, sub = row // 64 == colm // 64, row // 8 == colm // 8
    pair = np.concatenate([-1.0 * (sub & (row < colm)), -1.0 * (chunk & (row <= colm)),
                           1.0 * (chunk & (row < colm)), 1.0 * (chunk & (row <= colm))], axis=1)
    subm = np.concatenate([-1.0 * (sub & (colm < row)), -1.0 * (chunk & ~sub & (colm < row))], axis=1)
    sel = np.zeros((128, 8))
    sel[:, 0], sel[:, 1], sel[:, 2], sel[:, 3], sel[:, 4] = p < 64, p >= 64, 1, EPS, LNX_EPS
    return {
        "ident": np.eye(128, dtype=f),
        "idd": np.concatenate([np.eye(64), np.eye(64)]).astype(f),
        "blk64": (row // 64 == colm // 64).astype(f),
        "sel": sel.astype(f),
        "masks1": np.concatenate([causal, cmp_add, cmp_mul, pair, subm], axis=1).astype(f),
    }


def _units(w):
    m = w.shape[1] // 128
    return w.reshape(8, 128, m, 128).transpose(2, 1, 0, 3).reshape(m, 128, 1024)


def _down_units(w):
    w = np.concatenate([w, np.zeros((24 * 128 - FF, D), w.dtype)])
    return w.reshape(3, 8, 128, 8, 128).transpose(3, 0, 2, 1, 4).reshape(24, 128, 1024)


def _pad(w):
    return np.concatenate([w, np.zeros((w.shape[0], 128 - w.shape[1]), w.dtype)], axis=1)


def _pairs(a, b):
    return np.stack([_units(a), _units(b)], axis=1).reshape(-1, 128, 1024)


def _cols(v):
    return v.reshape(-1, 128).T


def _layout(a):
    heads = np.concatenate([np.concatenate([np.arange(64) + 64 * j, np.arange(64) + 64 * (4 + j)]) for j in range(4)])
    w = a["w_in"][0]
    at = np.cumsum([0, 512] + [128] * 6 + [24, 1792, 2048])
    q, kc, vc, ks, vs, kw, vw, gl, rw, mg = (w[:, at[n]:at[n + 1]] for n in range(10))
    proj = np.concatenate([a["proj_nsa"][0][heads], a["proj_rwkv"][0]])
    w2 = a["w_in_2"][0]
    up = a["ffn_up"][0]
    parts = [_units(q[:, heads]), _units(kc), _units(vc), _units(ks), _units(vs), _units(kw), _units(vw),
             _units(_pad(gl)), _units(rw), _units(mg), _units(proj), _units(a["w_out"][0]),
             _pairs(up[:, :FF], up[:, FF:]), _down_units(a["ffn_down"][0])]
    parts += _layout2(a, w2)
    conv = a["ffn_conv"][0].reshape(3, 2, KF, 128).transpose(3, 0, 2, 1).reshape(128, 3 * 2 * KF)
    dup = a["qk_gain"][0].T
    par = {"norm_mix": _cols(a["norm_mix"][0]), "norm_ffn": _cols(a["norm_ffn"][0]),
           "mu": _cols(a["rwkv_mu"][0]), "w0": _cols(a["rwkv_w0"][0]), "a0": _cols(a["rwkv_a0"][0]),
           "k_k": _cols(a["rwkv_k_k"][0]), "k_a": _cols(a["rwkv_k_a"][0]), "r_k": _cols(a["rwkv_r_k"][0].reshape(-1)),
           "ln_w": _cols(a["rwkv_ln_w"][0]), "ln_b": _cols(a["rwkv_ln_b"][0]),
           "qk_gain": np.concatenate([dup, dup]), "ffn_conv": conv,
           "ffn1_pre": _cols(a["ffn1_pre_g_2"][0]), "ffn1_post": _cols(a["ffn1_post_g_2"][0]),
           "mix_pre": _cols(a["mix_pre_g_2"][0]),
           "conv_w": a["conv_w_2"][0].reshape(4, 16, 128).transpose(2, 0, 1).reshape(128, 64),
           "conv_b": _cols(a["conv_b_2"][0]), "head_g": _cols(a["mlstm_head_g_2"][0]),
           "mix_post": _cols(a["mix_post_g_2"][0]), "ffn2_pre": _cols(a["ffn2_pre_g_2"][0]),
           "ffn2_post": _cols(a["ffn2_post_g_2"][0])}
    w1 = a["cmp_w1"][0].transpose(2, 0, 1, 3)
    pe = a["cmp_pe"][0].transpose(2, 0, 1)
    cw2 = a["cmp_w2"][0].transpose(1, 0, 2)
    lora = np.stack([np.concatenate([a["rwkv_w_up"][0], a["rwkv_a_up"][0]]), a["rwkv_g_up"][0]], axis=1)
    out = {"x": a["x"][0].T.reshape(8, 128, T).transpose(1, 0, 2), "w": np.concatenate(parts),
           "par": np.concatenate([par[n] for n, _ in PARAMS], axis=1),
           "cmp_w1": np.concatenate([w1, w1]), "cmp_pe": np.concatenate([pe, pe]),
           "cmp_w2": np.concatenate([cw2, cw2]), "lora": lora}
    out.update(_layout2_small(a))
    out.update(_shape_constants())
    return {n: np.ascontiguousarray(v, dtype=np.float32) for n, v in out.items()}


def kernel(**inputs):
    import concourse.bacc as bacc
    from concourse.bass_utils import run_bass_kernel_spmd

    arrays = _layout({n: np.asarray(v) for n, v in inputs.items()})
    nc = bacc.Bacc("TRN2", target_bir_lowering=False, num_devices=1)
    io = {n: nc.dram_tensor(f"in_{n}", v.shape, F32, kind="ExternalInput").ap() for n, v in arrays.items()}
    io["y"] = nc.dram_tensor("out_y", (128, KD, T), F32, kind="ExternalOutput").ap()
    build_program(nc, io)
    r = run_bass_kernel_spmd(nc, [{f"in_{n}": v for n, v in arrays.items()}], core_ids=[0])
    y = r.results[0]["out_y"]
    return np.ascontiguousarray(y.transpose(1, 0, 2).reshape(D, T).T)[None]


def _layout2(a, w2):
    cuts = np.cumsum([0, 1536, 1536, 1536, 1024, 1024, 1024, 1024, 4, 4, 1024, 1024])
    q, k, v, qm, km, vm, om, ip, fp, ga, gm = (w2[:, cuts[n]:cuts[n + 1]] for n in range(11))
    q, k, v, qm, km, vm, om, ga, gm = (_units(t) for t in (q, k, v, qm, km, vm, om, ga, gm))
    mix = []
    for h in range(4):
        mix += [t[4 * g + h] for t in (q, k, v) for g in range(3)] + [ga[2 * h], ga[2 * h + 1]]
    z = np.zeros((D, 28), w2.dtype)
    mix.append(_units(_pad(np.concatenate([ip, z, fp], axis=1)))[0])
    for h in range(4):
        mix += [t[2 * h + n] for t in (qm, km, vm, om, gm) for n in range(2)]
    watt = a["w_att_branch_2"][0].reshape(4, 128, 4, 2, 128).transpose(2, 1, 3, 0, 4).reshape(4, 128, 1024)
    wml = _units(a["w_mlstm_branch_2"][0]).reshape(4, 2, 128, 1024)
    branch = np.concatenate([watt[:, None], wml], axis=1).reshape(12, 128, 1024)
    return [_pairs(a["ffn1_w_gate_2"][0], a["ffn1_w_up_2"][0]), _down_units(a["ffn1_w_down_2"][0]),
            np.stack(mix), branch, _units(a["w_out_2"][0]),
            _pairs(a["ffn2_w_gate_2"][0], a["ffn2_w_up_2"][0]), _down_units(a["ffn2_w_down_2"][0])]


def _layout2_small(a):
    f = np.float32
    half = 16
    inv = np.power(f(500000.0), -(np.arange(half, dtype=f) * f(2.0) / f(32))).astype(f)
    ang = (np.arange(T, dtype=f)[None, :] * inv[:, None]).astype(f).astype(np.float64)
    cos, sin = np.cos(ang), np.sin(ang)
    rmat = np.zeros((128, 32))
    rmat[np.arange(16) + 16, np.arange(16)] = -1
    rmat[np.arange(16), np.arange(16) + 16] = 1
    m, s = np.arange(128)[:, None, None], np.arange(T)[None, None, :]
    r = np.arange(4)[None, :, None]
    dist = 4 * m + r - s
    ma = np.where((dist >= 0) & (dist <= 128), 0, NEG)
    d = np.arange(128)[:, None] - np.arange(128)[None, :]
    mb = np.broadcast_to(np.where(d >= 0, 0, NEG)[:, None, :], (128, 4, 128))
    mc = np.broadcast_to(np.where((d >= 0) & (d % 4 == 0), 0, NEG)[:, None, :], (128, 4, 128))
    sel4 = np.zeros((4, 4, T))
    sel4[np.arange(4), np.arange(4)] = 1
    return {"rope": np.stack([np.concatenate([cos, cos]), np.concatenate([sin, sin])], axis=1),
            "rmat": rmat, "mask2": np.concatenate([ma, mb, mc], axis=2),
            "mask_t": np.where(d <= 0, 0, NEG), "sel4": sel4, "ones": np.ones((128, 128)),
            "par_if": np.stack([a["mlstm_i_bias_2"][0], a["mlstm_f_bias_2"][0]], axis=1)}
```
